# Optimizing a Trainium2 kernel written in Bass

```python
import jax, jax.numpy as jnp
from jax import lax
import numpy as np

D_MODEL = 1024
BATCH = 1
SEQ = 512
DEPTH = 1

CHUNK = 64
Q_BLOCK = 128
N_BRANCH = 3
ATTN_HEADS = 8
ATTN_HEAD_DIM = 64
ATTN_WIDTH = ATTN_HEADS * ATTN_HEAD_DIM
POOL_WINDOWS = (2, 4, 8, 16)
POOL_GROUPS = 4
POOL_WIDTH = 512
POOL_GROUP_DIM = POOL_WIDTH // POOL_GROUPS
CONV_WIDTH = 512
CONV_K = 3
FFN_HIDDEN = -(-(8 * D_MODEL) // (3 * 256)) * 256
RMS_EPS = 1e-6
NEG_INF = -1e30

IN_SPLITS = (ATTN_WIDTH, ATTN_WIDTH, ATTN_WIDTH, ATTN_HEADS, POOL_WIDTH,
             CONV_WIDTH, CONV_WIDTH, CONV_WIDTH, N_BRANCH * D_MODEL)
IN_COLS = sum(IN_SPLITS)
IN_SPLIT_POINTS = tuple(int(p) for p in np.cumsum(IN_SPLITS)[:-1])

kernel_name = "hybrid_fox_pool_shortconv_gated_block"

def rms_norm(x, g):
    xf = x.astype(jnp.float32)
    y = xf * lax.rsqrt(jnp.mean(xf * xf, axis=-1, keepdims=True) + RMS_EPS)
    return (y * g.astype(jnp.float32)).astype(x.dtype)

def forgetting_attention(q, k, v, f_logit, b_f):
    B, S, H, Dh = q.shape
    log_f = jax.nn.log_sigmoid((f_logit + b_f).astype(jnp.float32))
    F = jnp.cumsum(log_f, axis=1)
    F_k = F.transpose(0, 2, 1)
    nblk = S // Q_BLOCK
    q_blocks = q.reshape(B, nblk, Q_BLOCK, H, Dh).swapaxes(0, 1)
    F_q_blocks = F.reshape(B, nblk, Q_BLOCK, H).swapaxes(0, 1)
    q_pos_blocks = jnp.arange(S, dtype=jnp.int32).reshape(nblk, Q_BLOCK)
    k_pos = jnp.arange(S, dtype=jnp.int32)
    scale = Dh ** -0.5

    def one_block(args):
        q_i, F_q_i, pos_i = args
        logits = jnp.einsum('bqhd,bkhd->bhqk', q_i, k).astype(jnp.float32) * scale
        decay = F_q_i.transpose(0, 2, 1)[..., :, None] - F_k[..., None, :]
        mask = k_pos[None, :] <= pos_i[:, None]
        logits = jnp.where(mask, logits + decay, NEG_INF)
        p = jax.nn.softmax(logits, axis=-1)
        return jnp.einsum('bhqk,bkhd->bqhd', p.astype(v.dtype), v)

    out = lax.map(one_block, (q_blocks, F_q_blocks, q_pos_blocks))
    return out.swapaxes(0, 1).reshape(B, S, H * Dh)

def multiscale_pool(u, pool_w, pool_scale):
    B, S, C = u.shape
    uf = u.astype(jnp.float32)
    c0 = jnp.pad(jnp.cumsum(uf, axis=1), ((0, 0), (1, 0), (0, 0)))
    n_avail = jnp.arange(1, S + 1, dtype=jnp.float32)[:, None]
    outs = []
    for g, w in enumerate(POOL_WINDOWS):
        sl = slice(g * POOL_GROUP_DIM, (g + 1) * POOL_GROUP_DIM)
        cg = c0[..., sl]
        lag = jnp.pad(cg, ((0, 0), (w, 0), (0, 0)))[:, :S + 1]
        mean = (cg - lag)[:, 1:] / jnp.minimum(n_avail, float(w))
        outs.append(mean - uf[..., sl])
    d = jnp.stack(outs, axis=2).astype(u.dtype)
    y = jnp.einsum('bsgc,gcd->bsgd', d, pool_w).reshape(B, S, C)
    return y * pool_scale

def short_gated_conv(v, gate_b, gate_c, conv_w):
    C = v.shape[-1]
    z = gate_c * v
    y = lax.conv_general_dilated(z, conv_w[:, None, :], window_strides=(1,),
                                 padding=[(CONV_K - 1, 0)],
                                 dimension_numbers=('NWC', 'WIO', 'NWC'),
                                 feature_group_count=C)
    return gate_b * y

def setup_inputs(seed: int = 0) -> dict:
    key = jax.random.key(seed)
    ks = jax.random.split(key, 18)
    f32 = jnp.float32

    def nrm(k, shape, fan_in):
        return jax.random.normal(k, shape, f32) * (fan_in ** -0.5)

    return {
        "x": jax.random.normal(ks[0], (BATCH, SEQ, D_MODEL), f32),
        "attn_norm": 1.0 + 0.05 * jax.random.normal(ks[1], (DEPTH, D_MODEL), f32),
        "w_in": nrm(ks[2], (DEPTH, D_MODEL, IN_COLS), D_MODEL),
        "b_forget": jax.random.uniform(ks[3], (DEPTH, ATTN_HEADS), f32, 1.0, 4.0),
        "b_gate": 0.1 * jax.random.normal(ks[4], (DEPTH, N_BRANCH * D_MODEL), f32),
        "w_proj_attn": nrm(ks[5], (DEPTH, ATTN_WIDTH, D_MODEL), ATTN_WIDTH),
        "pool_w": nrm(ks[6], (DEPTH, POOL_GROUPS, POOL_GROUP_DIM, POOL_GROUP_DIM), POOL_GROUP_DIM),
        "pool_scale": 1.0 + 0.1 * jax.random.normal(ks[7], (DEPTH, POOL_WIDTH), f32),
        "w_proj_pool": nrm(ks[8], (DEPTH, POOL_WIDTH, D_MODEL), POOL_WIDTH),
        "conv_w": nrm(ks[9], (DEPTH, CONV_K, CONV_WIDTH), CONV_K),
        "w_proj_conv": nrm(ks[10], (DEPTH, CONV_WIDTH, D_MODEL), CONV_WIDTH),
        "w_out": nrm(ks[11], (DEPTH, D_MODEL, D_MODEL), D_MODEL),
        "ffn_norm": 1.0 + 0.05 * jax.random.normal(ks[12], (DEPTH, D_MODEL), f32),
        "w_gate_up": nrm(ks[13], (DEPTH, D_MODEL, 2 * FFN_HIDDEN), D_MODEL),
        "w_down": nrm(ks[14], (DEPTH, FFN_HIDDEN, D_MODEL), FFN_HIDDEN),
        "final_norm": 1.0 + 0.05 * jax.random.normal(ks[15], (D_MODEL,), f32),
    }

def reference(x, attn_norm, w_in, b_forget, b_gate, w_proj_attn, pool_w, pool_scale,
              w_proj_pool, conv_w, w_proj_conv, w_out, ffn_norm, w_gate_up, w_down,
              final_norm):
    B, S, D = x.shape
    for l in range(DEPTH):
        h = rms_norm(x, attn_norm[l])
        proj = h @ w_in[l]
        q, k, v, f_logit, u, cv, cb, cc, g = jnp.split(proj, IN_SPLIT_POINTS, axis=-1)
        heads = (B, S, ATTN_HEADS, ATTN_HEAD_DIM)
        y_a = forgetting_attention(q.reshape(heads), k.reshape(heads), v.reshape(heads),
                                   f_logit, b_forget[l]) @ w_proj_attn[l]
        y_b = multiscale_pool(u, pool_w[l], pool_scale[l]) @ w_proj_pool[l]
        y_c = short_gated_conv(cv, cb, cc, conv_w[l]) @ w_proj_conv[l]
        gates = jax.nn.sigmoid(g + b_gate[l]).reshape(B, S, N_BRANCH, D)
        mixed = gates[..., 0, :] * y_a + gates[..., 1, :] * y_b + gates[..., 2, :] * y_c
        x = x + mixed @ w_out[l]
        h = rms_norm(x, ffn_norm[l])
        a, b = jnp.split(h @ w_gate_up[l], 2, axis=-1)
        x = x + (jax.nn.silu(a) * b) @ w_down[l]
    return rms_norm(x, final_norm)


_drawn_inputs = setup_inputs


def setup_inputs(seed=0):
    import zlib

    import numpy as np

    out = dict(_drawn_inputs(seed))
    spreads = {}
    factors = {}
    for name, (base, spread) in spreads.items():
        noise = np.random.default_rng([zlib.crc32(name.encode()), seed]).standard_normal(out[name].shape)
        drawn = base * np.exp(spread * noise) if base else spread * noise
        out[name] = __import__('jax').numpy.asarray(drawn.astype(out[name].dtype))
    for name, factor in factors.items():
        out[name] = (out[name] * factor).astype(out[name].dtype)
    return out
```

```python
from contextlib import ExitStack

import concourse.bass as bass
from concourse import mybir

ALU = mybir.AluOpType
ACT = mybir.ActivationFunctionType
F32 = mybir.dt.float32
F32R = mybir.dt.float32r
I32 = mybir.dt.int32
AX_X = mybir.AxisListType.X

P = 128
SLOTS = 3
UB = 8
EPS = 1e-6
NEG_INF = -1e30

STAGES = [("norm", 1, 0), ("front", 1, 5), ("pair", 4, 6), ("mix", 4, 9), ("out", 2, 3),
          ("out_end", 1, 2), ("ffn_first", 1, 2), ("ffn", 7, 6), ("down", 3, 6), ("down_end", 1, 6),
          ("end", 1, 0)]

RAISED = {
    "free0": dict(norm=1, front=2, pair=2, mix=2, out=1, out_end=1, ffn_first=1, ffn=1),
    "free1": dict(norm=1, front=2, pair=2, mix=2, out=1, out_end=1, ffn_first=1, ffn=1),
    "free2": dict(norm=1, front=1, pair=2, mix=2, out=1, ffn=1, down=1, down_end=1),
    "free3": dict(norm=1, front=5, pair=5, mix=2, out=1, out_end=1, ffn=1, down=1, down_end=1),
    "free4": dict(norm=1, front=2, pair=4, mix=2, out=1, out_end=1, ffn=1),
    "free5": dict(norm=1, front=2, pair=4, mix=1, out=1, ffn=1),
    "free6": dict(norm=1, front=2, pair=4, mix=1, ffn_first=1, down=1, down_end=1),
    "free7": dict(norm=2, front=2, pair=2, down=1, down_end=1),
    "full0": dict(norm=1), "full1": dict(norm=1), "full2": dict(norm=1),
    "full3": dict(norm=1, front=5, pair=5, out=1, out_end=1),
    "full4": dict(norm=1, front=2, pair=4, out=1, out_end=1),
    "full5": dict(norm=1, front=2, pair=4, out=1),
    "full6": dict(norm=1, front=2, pair=4, ffn_first=1, down=1, down_end=1),
    "full7": dict(norm=2, front=2, pair=2, down=1, down_end=1),
    "op_hi": dict(norm=8, front=8, pair=14, mix=2, out=3, out_end=2, ffn_first=1, ffn=3),
    "op_lo": dict(front=4, pair=1, mix=2, out=3, out_end=2, ffn_first=1, ffn=3),
    "scalar_tile": dict(norm=6, front=2, out=3, out_end=2, ffn_first=3, ffn=3, down=2, down_end=2,
                        end=4),
    "vector_tile": dict(norm=5, front=2, pair=1, mix=2, ffn_first=1, ffn=3, end=4),
    "row_max": dict(pair=2), "exp_done": dict(pair=2), "probs": dict(pair=2),
    "sumsq_done": dict(out=3, out_end=2),
    "vector_step": dict(norm=11, front=19, pair=15, mix=2, ffn_first=5, ffn=3, end=4),
}


def stage_of(name):
    first = 0
    for s, times, units in STAGES:
        if s == name:
            return first, units
        first += times * units


def count(what, stage, i, k):
    before = 0
    for s, times, _ in STAGES:
        if s == stage:
            return before + i * RAISED[what].get(s, 0) + k
        before += times * RAISED[what].get(s, 0)


def unit(stage, i, j):
    first, per = stage_of(stage)
    return first + j + i * per, (first + j) % SLOTS


def loads_before(stage, i, j):
    first, per = stage_of(stage)
    return (first + j) // SLOTS + 1 + i * (per // SLOTS)


def hybrid_block(nc, x, attn_norm, w_in, b_forget, b_gate, w_proj_attn, pool_w, pool_scale,
                 w_proj_pool, conv_w, w_proj_conv, w_out, ffn_norm, w_gate_up, w_down,
                 final_norm, out):
    x, out = x[0], out[0]
    S, D = x.shape
    H = b_forget.shape[1]
    AW = w_proj_attn.shape[1]
    HD = AW // H
    FH = w_down.shape[1]
    TB, DB, WB, FB = S // P, D // P, AW // P, FH // P
    POOL_WINDOWS = (2, 4, 8, 16)
    PAD = max(POOL_WINDOWS)
    SCALE = float(HD) ** -0.5
    w_in, w_out, w_gate_up, w_down = w_in[0], w_out[0], w_gate_up[0], w_down[0]
    w_proj = [w_proj_attn[0], w_proj_pool[0], w_proj_conv[0]]
    conv_k = conv_w.shape[1]
    COL_Q, COL_K, COL_V, COL_F = 0, AW, 2 * AW, 3 * AW
    COL_U = COL_F + H
    COL_CV, COL_CB, COL_CC = COL_U + AW, COL_U + 2 * AW, COL_U + 3 * AW
    COL_G = COL_U + 4 * AW

    V_ATTN, V_FFN, V_GATE = 0, DB, 2 * DB
    V_SCALE = V_GATE + 3 * DB
    V_CONV = V_SCALE + WB
    N_VECS = V_CONV + conv_k * WB

    with ExitStack() as ctx:
        def sb(name, shape, dt=F32):
            return ctx.enter_context(nc.sbuf_tensor(name, shape, dt))

        def sem(name):
            return ctx.enter_context(nc.semaphore(name))

        operands = sb("operands", [P, (DB + FB) * 2 * S], F32R)
        raw = sb("raw", [P, SLOTS, UB * P])
        whi = sb("whi", [P, SLOTS, UB * P], F32R)
        wlo = sb("wlo", [P, SLOTS, UB * P], F32R)
        big_x = sb("big_x", [P, DB * S])
        big_y = sb("big_y", [P, DB * S])
        work = sb("work", [P, 3072])
        ident = sb("ident", [P, P])
        mask = sb("mask", [P, P])
        ones = sb("ones", [P, S])
        vecs = sb("vecs", [P, N_VECS])
        inv16 = sb("inv16", [P, 4, PAD])
        steps16 = sb("steps16", [P, PAD], I32)
        recip16 = sb("recip16", [P, PAD])
        edge = sb("edge", [P, PAD])
        f_rows = sb("f_rows", [P, TB, H])
        stat = sb("stat", [P, 64])
        bias_f = sb("bias_f", [H, 1])

        def opnd(at, blocks):
            return at, at + blocks * S

        H_HI, H_LO = opnd(0, DB)
        BR = [opnd(2 * DB * S + 2 * WB * S * b, WB) for b in range(3)]
        T0 = 2 * DB * S + 6 * WB * S
        Q_HI, Q_LO, K_HI, K_LO, V_HI, V_LO = [T0 + S * j for j in range(6)]
        PT_COLS = S * (TB + 1) // 2
        PT = [(T0 + 6 * S + 2 * PT_COLS * a, T0 + 6 * S + 2 * PT_COLS * a + PT_COLS)
              for a in range(2)]
        PW_HI, PW_LO, DF_HI, DF_LO = [T0 + 6 * S + 4 * PT_COLS + S * j for j in range(4)]
        F_HI, F_LO, SEL = PT[0][0], PT[0][0] + S, PT[0][0] + 2 * S
        MX_HI, MX_LO = opnd(T0, DB)
        HID_HI, HID_LO = opnd(2 * DB * S, FB)

        def op(at, n=S, rows=slice(0, P)):
            return operands[rows, at:at + n]

        def opd(at, index, n=S):
            return operands[:, bass.ds(at + index * S, n)]

        def wk(slot, n=S, rows=slice(0, P)):
            return work[rows, slot * S:slot * S + n]

        VT, CV, CB, CY = 0, 1, 2, 3
        GA, ACC, TMP = 0, 3, 4
        XS, XT, SQ = 0, 3, 4
        A1, SG, B1, HD_ = 0, 1, 2, 3
        X2, JUNK, FG = 0, 2, 4
        cum = work[:, 0:PAD + S]
        diff = work[:, PAD + S:PAD + 2 * S]
        fz = work[0:H, PAD + 2 * S:PAD + 3 * S]
        fe = work[0:H, PAD + 3 * S:PAD + 4 * S]
        fF = work[0:H, PAD + 4 * S:PAD + 5 * S]
        vec_rows = work[0:N_VECS, PAD + 5 * S:PAD + 5 * S + P]
        pw_raw = big_y[:, 0:4 * P]
        L_AT = [0, 3 * P, 6 * P, 9 * P]
        L_COLS = 13 * P
        PT_AT = [0, 4 * P, 7 * P, 9 * P]
        SUMSQ, VAR, RSTD = [big_y[:, j * S:(j + 1) * S] for j in range(3)]
        ytok = big_y[:].rearrange("p (t d) -> p t d", t=TB)
        final_g = work[:, FG * S:FG * S + D]

        banks = [ctx.enter_context(nc.psum_tensor(f"bank{b}", [P, S], F32)) for b in range(8)]

        x_in = [sem(f"x_in{t}") for t in range(TB)]
        const_in = sem("const_in")
        pool_w_in = sem("pool_w_in")
        xs_in = [sem(f"xs_in{j}") for j in range(3)]
        final_g_in = sem("final_g_in")
        landed = [sem(f"landed{s}") for s in range(SLOTS)]
        loads_begun = sem("loads_begun")
        w_hi = sem("w_hi")
        w_lo = sem("w_lo")
        used = sem("used")
        full = [sem(f"full{b}") for b in range(8)]
        free = [sem(f"free{b}") for b in range(8)]
        sumsq_done = sem("sumsq_done")
        op_hi, op_lo = sem("op_hi"), sem("op_lo")
        scalar_tile, vector_tile = sem("scalar_tile"), sem("vector_tile")
        row_max, exp_done, probs = sem("row_max"), sem("exp_done"), sem("probs")
        vector_step = sem("vector_step")
        consts = sem("consts")
        pool_w_hi, pool_w_lo = sem("pool_w_hi"), sem("pool_w_lo")
        stored = sem("stored")

        def wait_full(eng, b, stage, i, k):
            eng.wait_ge(full[b], count(f"full{b}", stage, i, k))

        def wait_unit(eng, stage, i, j):
            eng.wait_ge(used, unit(stage, i, j)[0] + 1)

        def wait_free(eng, b, stage, i, k):
            eng.wait_ge(free[b], count(f"free{b}", stage, i, k))

        block = ctx.enter_context(nc.Block())

        @block.sync
        def _(sp):
            def load(stage, i, j, halves):
                n, s = unit(stage, i, j)
                if not (stage == "front" and n < SLOTS):
                    sp.wait_ge(w_lo, n - SLOTS + 1)
                    sp.sem_inc(loads_begun, 1)
                for src, at in halves:
                    nb = src.shape[0] // P
                    dst = raw[:, s, at * P:(at + nb) * P].rearrange("p (k c) -> p k c", c=P)
                    sp.dma_start(dst, src.rearrange("(k p) c -> p k c", p=P)
                                 ).then_inc(landed[s], 16)

            def columns(w, col, rows=0, nb=8):
                h = (nb + 1) // 2 if nb != 6 else 4
                c = bass.ds(col, P)
                return [(w[rows:rows + h * P, c], 0), (w[rows + h * P:rows + nb * P, c], h)]

            for t in range(TB):
                sp.dma_start(big_x[:, t * D:(t + 1) * D], x[t * P:(t + 1) * P, :]
                             ).then_inc(x_in[t], 16)
            for src, at in ((attn_norm, V_ATTN), (ffn_norm, V_FFN), (b_gate, V_GATE),
                            (pool_scale, V_SCALE)):
                r = src[0].rearrange("(r c) -> r c", c=P)
                sp.dma_start(vec_rows[at:at + r.shape[0], :], r).then_inc(const_in, 16)
            sp.dma_start(vec_rows[V_CONV:N_VECS, :],
                         conv_w[0].rearrange("k (r c) -> (k r) c", c=P)).then_inc(const_in, 16)
            sp.dma_start(bias_f[:], b_forget[0].rearrange("(h a) -> h a", a=1)
                         ).then_inc(const_in, 16)

            front = [COL_F] + [COL_U + g * P for g in range(4)]
            for j in range(3):
                load("front", 0, j, columns(w_in, front[j]))
            sp.wait_ge(full[DB - 2], count(f"full{DB - 2}", "norm", 0, 1))
            sp.wait_ge(full[DB - 1], count(f"full{DB - 1}", "norm", 0, 2))
            sp.dma_start(pw_raw.rearrange("p (g d) -> p g d", g=4),
                         pool_w[0].rearrange("g c d -> c g d")).then_inc(pool_w_in, 16)
            for j in range(3, 5):
                load("front", 0, j, columns(w_in, front[j]))
            with sp.Fori(0, WB) as i:
                for j, col in enumerate((COL_Q, COL_K, COL_V, COL_CV, COL_CB, COL_CC)):
                    load("pair", i, j, columns(w_in, i * P + col))

            with sp.Fori(0, DB // 2) as i:
                def gate(j, br, mm):
                    load("mix", i, j, columns(w_in, i * (2 * P) + (COL_G + br * D + mm * P)))

                def proj(j, first, second):
                    load("mix", i, j,
                         [(w_proj[br][:, bass.ds(i * (2 * P) + mm * P, P)], at)
                          for (br, mm), at in ((first, 0), (second, WB))])

                gate(0, 0, 0)
                gate(1, 1, 0)
                proj(2, (0, 0), (1, 0))
                gate(3, 2, 0)
                proj(4, (2, 0), (2, 1))
                gate(5, 0, 1)
                gate(6, 1, 1)
                proj(7, (0, 1), (1, 1))
                gate(8, 2, 1)

            def out_loads(stage, i, m0, nm):
                for j in range(nm):
                    load(stage, i, j, columns(w_out, m0(i, j)))
                for j in range(nm):
                    if stage == "out":
                        sp.wait_ge(op_lo, count("op_lo", "mix", 3, 2))
                        sp.wait_ge(full[3 + j], count(f"full{3 + j}", "out", i, 0))
                    else:
                        sp.wait_ge(full[3 + j], count(f"full{3 + j}", "out", 1, 1))
                    sp.sem_inc(loads_begun, 1)
                    sp.dma_start(wk(XS + j).rearrange("p (t c) -> p t c", c=P),
                                 x.rearrange("(t p) c -> p t c", p=P)[:, :, bass.ds(m0(i, j), P)]
                                 ).then_inc(xs_in[j], 16)

            with sp.Fori(0, 2) as i:
                out_loads("out", i, lambda i, j: i * (3 * P) + j * P, 3)
            out_loads("out_end", 0, lambda i, j: (6 + j) * P, 2)

            load("ffn_first", 0, 0, columns(w_gate_up, 0))
            load("ffn_first", 0, 1, columns(w_gate_up, FH))
            with sp.Fori(0, 7) as i:
                for j in range(3):
                    load("ffn", i, 2 * j, columns(w_gate_up, i * (3 * P) + (1 + j) * P))
                    load("ffn", i, 2 * j + 1, columns(w_gate_up, i * (3 * P) + (1 + j) * P + FH))

            sp.wait_ge(sumsq_done, DB + 1)
            sp.dma_start(final_g, final_norm.rearrange("(a d) -> a d", a=1).to_broadcast([P, D])
                         ).then_inc(final_g_in, 16)

            def down_loads(stage, i, col):
                for mm in range(2):
                    for c in range(3):
                        nb = 8 if c < 2 else FB - 16
                        load(stage, i, 3 * mm + c, columns(w_down, col + mm * P, c * 8 * P, nb))

            with sp.Fori(0, 3) as i:
                down_loads("down", i, i * (2 * P))
            down_loads("down_end", 0, 6 * P)

            for t in range(TB):
                if t % 2 == 0:
                    sp.wait_ge(vector_tile, count("vector_tile", "end", 0, 3 + t // 2))
                else:
                    sp.wait_ge(scalar_tile, count("scalar_tile", "end", 0, 3 + t // 2))
                sp.dma_start(out[t * P:(t + 1) * P, :], ytok[:, t, :]).then_inc(stored, 16)
            sp.wait_ge(stored, 16 * TB)

        @block.gpsimd
        def _(pool):
            nc.gpsimd.memset(ident[:], 0.0).then_inc(consts, 1)
            nc.gpsimd.memset(mask[:], 0.0).then_inc(consts, 1)
            nc.gpsimd.memset(op(SEL, H * P, slice(0, H)).bitcast(F32), 0.0).then_inc(consts, 1)
            nc.gpsimd.memset(ones[:], 1.0).then_inc(consts, 1)
            pool.wait_ge(consts, 4)
            nc.gpsimd.affine_select(out=ident[:], in_=ident[:], compare_op=ALU.not_equal, fill=1.0,
                                    base=0, pattern=[[-1, P]], channel_multiplier=1
                                    ).then_inc(consts, 1)
            nc.gpsimd.affine_select(out=mask[:], in_=mask[:], compare_op=ALU.is_ge, fill=NEG_INF,
                                    base=0, pattern=[[-1, P]], channel_multiplier=1
                                    ).then_inc(consts, 1)
            sel = op(SEL, H * P, slice(0, H)).rearrange("p (h c) -> p h c", h=H)
            nc.gpsimd.affine_select(out=sel, in_=sel.bitcast(F32), compare_op=ALU.not_equal,
                                    fill=-1.0, base=0, pattern=[[-1, H], [0, P]],
                                    channel_multiplier=1).then_inc(consts, 1)
            nc.gpsimd.iota(steps16[:], pattern=[[1, PAD]], base=1, channel_multiplier=0
                           ).then_inc(consts, 1)

        @block.tensor
        def _(pe):
            def begin(b, stage, i, k):
                before = count(f"free{b}", stage, i, k - 1)
                if not (isinstance(before, int) and before == 0):
                    pe.wait_ge(free[b], before)

            def product(b, s, blocks, hi, lo, first, last, width=S, ready=None):
                for n, (wb, k) in enumerate(blocks):
                    if ready is not None:
                        ready(k)
                    w = slice(wb * P, (wb + 1) * P)
                    a, z = first and n == 0, last and n == len(blocks) - 1
                    nc.tensor.matmul(banks[b][:, 0:width], whi[:, s, w], op(hi + k * S),
                                     start=a, stop=False)
                    nc.tensor.matmul(banks[b][:, 0:width], whi[:, s, w], op(lo + k * S),
                                     start=False, stop=False)
                    mm = nc.tensor.matmul(banks[b][:, 0:width], wlo[:, s, w], op(hi + k * S),
                                          start=False, stop=z)
                return mm

            def unit_ready(stage, i, j):
                n, s = unit(stage, i, j)
                pe.wait_ge(w_lo, n + 1)
                return s

            def whole(b, stage, i, j, k, hi, lo, ready=None):
                s = unit_ready(stage, i, j)
                begin(b, stage, i, k)
                mm = product(b, s, [(c, c) for c in range(UB)], hi, lo, True, True, ready=ready)
                mm.then_inc(used, 1)

            pe.wait_ge(const_in, 16 * 6)
            pe.wait_ge(consts, 8)
            nc.tensor.transpose(banks[7][:, 0:N_VECS], vec_rows, ident[0:N_VECS, 0:N_VECS]
                                ).then_inc(full[7], 1)
            begin(7, "norm", 0, 2)
            for t in range(TB):
                pe.wait_ge(vector_tile, count("vector_tile", "norm", 0, 2 + t))
                for k in range(DB):
                    tr = nc.tensor.transpose(banks[k][:, t * P:(t + 1) * P],
                                             big_y[:, t * D + k * P:t * D + (k + 1) * P], ident[:])
                    if t == TB - 1:
                        tr.then_inc(full[k], 1)

            def h_ready(k):
                wait_free(pe, k, "norm", 0, 1 if k < 7 else 2)

            def pool_map(g):
                pe.wait_ge(op_lo, count("op_lo", "front", 0, g + 1))
                if g == 0:
                    pe.wait_ge(pool_w_lo, 1)
                begin(3, "front", 0, g + 1 if g < 3 else 5)
                w = slice(g * P, (g + 1) * P)
                nc.tensor.matmul(banks[3][:], op(PW_HI)[:, w], op(DF_HI), start=True, stop=False)
                nc.tensor.matmul(banks[3][:], op(PW_HI)[:, w], op(DF_LO), start=False, stop=False)
                nc.tensor.matmul(banks[3][:], op(PW_LO)[:, w], op(DF_HI), start=False, stop=True
                                 ).then_inc(full[3], 1)

            whole(0, "front", 0, 0, 1, H_HI, H_LO, h_ready)
            whole(1, "front", 0, 1, 1, H_HI, H_LO)
            whole(2, "front", 0, 2, 1, H_HI, H_LO)
            pool_map(0)
            whole(0, "front", 0, 3, 2, H_HI, H_LO)
            pool_map(1)
            whole(1, "front", 0, 4, 2, H_HI, H_LO)
            pool_map(2)
            pe.wait_ge(vector_tile, count("vector_tile", "front", 0, 2))
            begin(3, "front", 0, 4)
            for t in range(TB):
                tr = nc.tensor.transpose(banks[3][:, t * H:(t + 1) * H], fF[:, t * P:(t + 1) * P],
                                         ident[0:H, 0:H])
            tr.then_inc(full[3], 1)
            for h in range(H):
                b = 4 + h % 4
                begin(b, "front", 0, h // 4 + 1)
                sel = op(SEL + h * P, P, slice(0, H))
                nc.tensor.matmul(banks[b][:], sel, op(F_HI, S, slice(0, H)), start=True, stop=False)
                nc.tensor.matmul(banks[b][:], sel, op(F_LO, S, slice(0, H)), start=False, stop=True
                                 ).then_inc(full[b], 1)
            pool_map(3)

            with pe.Fori(0, WB) as i:
                whole(0, "pair", i, 0, 1, H_HI, H_LO)
                whole(1, "pair", i, 1, 1, H_HI, H_LO)
                wait_free(pe, 0, "pair", i, 1)
                wait_free(pe, 1, "pair", i, 1)
                for a in range(2):
                    rows = slice(a * HD, (a + 1) * HD)
                    for b in range(TB):
                        begin(3 + b, "pair", i, a + 1)
                        n = (b + 1) * P
                        dst = banks[3 + b][:, 0:n]
                        nc.tensor.matmul(dst, op(Q_HI + b * P, P, rows), op(K_HI, n, rows),
                                         start=True, stop=False)
                        nc.tensor.matmul(dst, op(Q_HI + b * P, P, rows), op(K_LO, n, rows),
                                         start=False, stop=False)
                        nc.tensor.matmul(dst, op(Q_LO + b * P, P, rows), op(K_HI, n, rows),
                                         start=False, stop=True).then_inc(full[3 + b], 1)
                whole(2, "pair", i, 2, 1, H_HI, H_LO)
                whole(0, "pair", i, 3, 2, H_HI, H_LO)
                wait_free(pe, 2, "pair", i, 1)
                begin(7, "pair", i, 1)
                for t in range(TB):
                    tr = nc.tensor.transpose(banks[7][:, t * P:(t + 1) * P],
                                             wk(VT)[:, t * P:(t + 1) * P], ident[:])
                tr.then_inc(full[7], 1)
                whole(1, "pair", i, 4, 2, H_HI, H_LO)

                def turn_probs(a):
                    pe.wait_ge(probs, count("probs", "pair", i, a + 1))
                    for j in range(TB):
                        begin(3 + j, "pair", i, 3 + a)
                        for b in range(j, TB):
                            at = a * L_COLS + L_AT[b] + j * P
                            tr = nc.tensor.transpose(banks[3 + j][:, b * P:(b + 1) * P],
                                                     big_y[:, at:at + P], ident[:])
                        tr.then_inc(full[3 + j], 1)

                turn_probs(0)
                s = unit_ready("pair", i, 5)
                begin(2, "pair", i, 2)
                product(2, s, [(c, c) for c in range(4)], H_HI, H_LO, True, False)
                turn_probs(1)
                product(2, s, [(c, c) for c in range(4, 8)], H_HI, H_LO, False, True
                        ).then_inc(used, 1)

                for a, b, k in ((0, 7, 2), (1, 3, 5)):
                    wait_free(pe, 7, "pair", i, 1)
                    for j in range(TB):
                        wait_free(pe, 3 + j, "pair", i, 3 + a)
                    begin(b, "pair", i, k)
                    for j in range(TB):
                        dst = banks[b][:, j * P:S]
                        n, at = S - j * P, PT_AT[j]
                        vj = slice(j * P, (j + 1) * P)
                        nc.tensor.matmul(dst, op(V_HI)[:, vj], op(PT[a][0] + at, n),
                                         start=(j == 0), stop=False)
                        nc.tensor.matmul(dst, op(V_HI)[:, vj], op(PT[a][1] + at, n),
                                         start=False, stop=False)
                        mm = nc.tensor.matmul(dst, op(V_LO)[:, vj], op(PT[a][0] + at, n),
                                              start=False, stop=(j == TB - 1))
                    mm.then_inc(full[b], 1)

            with pe.Fori(0, DB // 2) as i:
                pe.wait_ge(op_lo, count("op_lo", "pair", 3, 1))
                wait_free(pe, 7, "pair", 3, 2)
                wait_free(pe, 3, "pair", 3, 5)

                def project(j, parts):
                    s = unit_ready("mix", i, j)
                    for half, (br, b, k) in enumerate(parts):
                        begin(b, "mix", i, k)
                        mm = product(b, s, [(half * WB + c, c) for c in range(WB)], *BR[br],
                                     True, True)
                    mm.then_inc(used, 1)

                whole(0, "mix", i, 0, 1, H_HI, H_LO)
                whole(1, "mix", i, 1, 1, H_HI, H_LO)
                project(2, [(0, 3, 1), (1, 4, 1)])
                whole(2, "mix", i, 3, 1, H_HI, H_LO)
                project(4, [(2, 5, 1), (2, 6, 1)])
                whole(0, "mix", i, 5, 2, H_HI, H_LO)
                whole(1, "mix", i, 6, 2, H_HI, H_LO)
                project(7, [(0, 3, 2), (1, 4, 2)])
                whole(2, "mix", i, 8, 2, H_HI, H_LO)

            def out_block(stage, i, j, loads):
                pe.wait_ge(xs_in[j], loads)
                begin(3 + j, stage, i, 1)
                for t in range(TB):
                    tr = nc.tensor.transpose(banks[3 + j][:, t * P:(t + 1) * P],
                                             wk(XS + j)[:, t * P:(t + 1) * P], ident[:])
                tr.then_inc(full[3 + j], 1)

                def merged(k):
                    if k == DB - 1:
                        pe.wait_ge(op_lo, count("op_lo", "mix", 3, 2))
                    elif k == 0:
                        pe.wait_ge(op_lo, count("op_lo", "mix", 3, 1))

                whole(j, stage, i, j, 1, MX_HI, MX_LO, merged)

            with pe.Fori(0, 2) as i:
                for j in range(3):
                    out_block("out", i, j, i * 16 + 16)
            for j in range(2):
                out_block("out_end", 0, j, 48)

            def x1_ready(k):
                if k < 6:
                    pe.wait_ge(op_lo, count("op_lo", "out", 1, 3))
                else:
                    pe.wait_ge(op_lo, count("op_lo", "out_end", 0, k - 5))

            whole(0, "ffn_first", 0, 0, 1, H_HI, H_LO, x1_ready)
            pe.wait_ge(sumsq_done, DB + 1)
            begin(6, "ffn_first", 0, 1)
            nc.tensor.matmul(banks[6][:], ones[:, 0:P], SUMSQ, start=True, stop=True
                             ).then_inc(full[6], 1)
            whole(1, "ffn_first", 0, 1, 1, H_HI, H_LO)
            with pe.Fori(0, 7) as i:
                for j in range(3):
                    a = (2 * j + 2) % 6
                    whole(a, "ffn", i, 2 * j, 1, H_HI, H_LO)
                    whole(a + 1, "ffn", i, 2 * j + 1, 1, H_HI, H_LO)

            def down_pair(stage, i):
                def part(b, j, c):
                    s = unit_ready(stage, i, j)
                    nb = 8 if c < 2 else FB - 16
                    if c == 0:
                        begin(b, stage, i, 1)
                    mm = product(b, s, [(q, c * 8 + q) for q in range(nb)], HID_HI, HID_LO,
                                 c == 0, c == 2)
                    mm.then_inc(used, 1)

                def turn(mm):
                    wait_free(pe, 2 + mm, stage, i, 1)
                    begin(6 + mm, stage, i, 1)
                    for t in range(TB):
                        tr = nc.tensor.transpose(banks[6 + mm][:, t * P:(t + 1) * P],
                                                 wk(X2 + mm)[:, t * P:(t + 1) * P], ident[:])
                    tr.then_inc(full[6 + mm], 1)

                pe.wait_ge(op_lo, count("op_lo", "ffn", 6, 3))
                for c in range(3):
                    part(2, c, c)
                part(3, 3, 0)
                turn(0)
                part(3, 4, 1)
                part(3, 5, 2)
                turn(1)

            with pe.Fori(0, 3) as i:
                down_pair("down", i)
            down_pair("down_end", 0)

        @block.scalar
        def _(act):
            def split_hi(stage, i, j):
                n, s = unit(stage, i, j)
                act.wait_ge(landed[s], 32 * loads_before(stage, i, j))
                if not (stage == "front" and n < SLOTS):
                    act.wait_ge(used, n - SLOTS + 1)
                nc.scalar.copy(whi[:, s, :], raw[:, s, :]).then_inc(w_hi, 1)

            def operand_hi(dst, src, scale=1.0):
                nc.scalar.activation(dst, src, ACT.Copy, scale=scale).then_inc(op_hi, 1)

            def tile(dst, src, func, **kw):
                return nc.scalar.activation(dst, src, func, **kw).then_inc(scalar_tile, 1)

            for t in range(TB):
                act.wait_ge(x_in[t], 16)
                tile(big_y[:, t * D:(t + 1) * D], big_x[:, t * D:(t + 1) * D], ACT.Square,
                     accum_out=stat[:, t:t + 1])
            act.wait_ge(vector_tile, count("vector_tile", "norm", 0, 1))
            tile(stat[:, 8:12], stat[:, 4:8], ACT.Ln)
            act.wait_ge(scalar_tile, count("scalar_tile", "norm", 0, 5))
            tile(stat[:, 12:16], stat[:, 8:12], ACT.Exp, scale=-0.5)
            split_hi("front", 0, 0)
            wait_free(act, 7, "norm", 0, 1)
            for k in range(DB):
                wait_full(act, k, "norm", 0, 1 if k < 7 else 2)
                operand_hi(op(H_HI + k * S), banks[k][:], vecs[:, V_ATTN + k:V_ATTN + k + 1])
                if k == 3:
                    split_hi("front", 0, 1)
            split_hi("front", 0, 2)
            split_hi("front", 0, 3)
            act.wait_ge(vector_tile, count("vector_tile", "front", 0, 1))
            tile(fe, fe, ACT.Exp, scale=-1.0)
            act.wait_ge(scalar_tile, count("scalar_tile", "front", 0, 1))
            tile(fe, fe, ACT.Ln, bias=1.0)
            act.wait_ge(pool_w_in, 16)
            nc.scalar.copy(op(PW_HI), pw_raw).then_inc(pool_w_hi, 1)

            def pool_out(g):
                wait_full(act, 3, "front", 0, g + 1 if g < 3 else 5)
                operand_hi(op(BR[1][0] + g * S), banks[3][:], vecs[:, V_SCALE + g:V_SCALE + g + 1])

            for g in range(4):
                split_hi("front", 0, 4 + g)
                if g > 0:
                    pool_out(g - 1)
                wait_free(act, (1, 2, 0, 1)[g], "front", 0, (1, 1, 2, 2)[g])
                operand_hi(op(DF_HI), diff)
            for h in range(H):
                b = 4 + h % 4
                wait_full(act, b, "front", 0, h // 4 + 1)
                nc.scalar.copy(big_x[:, h * S:(h + 1) * S], banks[b][:]).then_inc(free[b], 1)
            pool_out(3)

            with act.Fori(0, WB) as i:
                split_hi("pair", i, 3)
                wait_unit(act, "pair", i, 0)
                operand_hi(op(Q_HI), banks[0][:], SCALE)
                split_hi("pair", i, 4)
                wait_unit(act, "pair", i, 1)
                operand_hi(op(K_HI), banks[1][:])
                for a in range(2):
                    act.wait_ge(row_max, count("row_max", "pair", i, a + 1))
                    for b in range(TB):
                        lg = big_y[:, a * L_COLS + L_AT[b]:a * L_COLS + L_AT[b] + (b + 1) * P]
                        at = 4 * a + b
                        e = nc.scalar.activation(lg, lg, ACT.Exp, bias=stat[:, 16 + at:17 + at],
                                                 accum_out=stat[:, 24 + at:25 + at])
                    e.then_inc(exp_done, 1)
                split_hi("pair", i, 5)
                wait_unit(act, "pair", i, 2)
                nc.scalar.copy(wk(VT), banks[2][:]).then_inc(free[2], 1)
                split_hi("pair", i, 6)
                wait_unit(act, "pair", i, 3)
                nc.scalar.copy(wk(CV), banks[0][:]).then_inc(free[0], 1)
                wait_full(act, 7, "pair", i, 1)
                operand_hi(op(V_HI), banks[7][:])
                split_hi("pair", i, 7)
                wait_unit(act, "pair", i, 4)
                nc.scalar.copy(wk(CB), banks[1][:]).then_inc(free[1], 1)
                for a in range(2):
                    for j in range(TB):
                        wait_full(act, 3 + j, "pair", i, 3 + a)
                        operand_hi(op(PT[a][0] + PT_AT[j], S - j * P), banks[3 + j][:, j * P:S])
                split_hi("pair", i, 8)
                for a, b, k in ((0, 7, 2), (1, 3, 5)):
                    rows = slice(a * HD, (a + 1) * HD)
                    wait_full(act, b, "pair", i, k)
                    operand_hi(operands[rows, bass.ds(BR[0][0] + i * S, S)], banks[b][rows, :])
                act.wait_ge(vector_tile, count("vector_tile", "pair", i, 1))
                operand_hi(opd(BR[2][0], i), wk(CY))

            with act.Fori(0, DB // 2) as i:
                def gate(j, b, k, br, mm):
                    wait_unit(act, "mix", i, j)
                    if mm == 0:
                        wait_free(act, (3, 4, 6)[br], "mix", i, 0)
                    else:
                        wait_free(act, (3, 4, 5)[br], "mix", i, 1)
                    nc.scalar.activation(wk(GA + br), banks[b][:], ACT.Sigmoid,
                                         bias=vecs[:, bass.ds(i * 2 + (V_GATE + br * DB + mm), 1)]
                                         ).then_inc(free[b], 1)

                def merged_hi(mm):
                    act.wait_ge(vector_tile, count("vector_tile", "mix", i, mm + 1))
                    operand_hi(opd(MX_HI, i * 2 + mm), wk(ACC))

                split_hi("mix", i, 3)
                gate(0, 0, 1, 0, 0)
                split_hi("mix", i, 4)
                gate(1, 1, 1, 1, 0)
                split_hi("mix", i, 5)
                split_hi("mix", i, 6)
                gate(3, 2, 1, 2, 0)
                split_hi("mix", i, 7)
                merged_hi(0)
                split_hi("mix", i, 8)
                gate(5, 0, 2, 0, 1)
                split_hi("mix", i, 9)
                gate(6, 1, 2, 1, 1)
                split_hi("mix", i, 10)
                split_hi("mix", i, 11)
                gate(8, 2, 2, 2, 1)
                merged_hi(1)

            def out_block(stage, i, j, m, nm):
                split_hi(stage, i, j + 3)
                wait_full(act, 3 + j, stage, i, 1)
                nc.scalar.copy(wk(XT), banks[3 + j][:]).then_inc(free[3 + j], 1)
                act.wait_ge(sumsq_done, count("sumsq_done", stage, i, j) + 1)
                wait_free(act, j, stage, i, 1)
                x1 = big_x[:, bass.ds(m * S, S)]
                operand_hi(opd(H_HI, m), x1, vecs[:, bass.ds(m + V_FFN, 1)])
                tile(wk(SQ), x1, ACT.Square)

            with act.Fori(0, 2) as i:
                for j in range(3):
                    out_block("out", i, j, i * 3 + j, 3)
            for j in range(2):
                out_block("out_end", 0, j, 6 + j, 2)

            def hidden(stage, i, j, a):
                if stage == "ffn":
                    split_hi(stage, i, 2 * j + 3)
                wait_free(act, a, stage, i, 1)
                tile(wk(SG), wk(A1), ACT.Sigmoid)
                split_hi(stage, i, 2 * j + 4)
                act.wait_ge(vector_tile, count("vector_tile", stage, i, j + 1))
                hb = i * 3 + (1 + j) if stage == "ffn" else 0
                operand_hi(opd(HID_HI, hb), wk(HD_))

            split_hi("ffn_first", 0, 3)
            wait_free(act, 6, "ffn_first", 0, 1)
            tile(RSTD, VAR, ACT.Ln)
            act.wait_ge(scalar_tile, count("scalar_tile", "ffn_first", 0, 1))
            tile(RSTD, RSTD, ACT.Exp, scale=-0.5)
            hidden("ffn_first", 0, 0, 0)
            with act.Fori(0, 7) as i:
                for j in range(3):
                    hidden("ffn", i, j, (2 * j + 2) % 6)

            def squares(stage, i, mm, m):
                wait_full(act, 6 + mm, stage, i, 1)
                for t in range(TB):
                    sq = nc.scalar.activation(wk(JUNK)[:, t * P:(t + 1) * P],
                                              banks[6 + mm][:, t * P:(t + 1) * P], ACT.Square,
                                              accum_out=stat[:, bass.ds(m + (16 + t * DB), 1)])
                sq.then_inc(scalar_tile, 1)

            with act.Fori(0, 3) as i:
                for j in range(3, 7):
                    split_hi("down", i, j)
                squares("down", i, 0, i * 2)
                split_hi("down", i, 7)
                split_hi("down", i, 8)
                squares("down", i, 1, i * 2 + 1)
            for j in range(3, 6):
                split_hi("down_end", 0, j)
            squares("down_end", 0, 0, 6)
            squares("down_end", 0, 1, 7)

            act.wait_ge(vector_tile, count("vector_tile", "end", 0, 1))
            tile(stat[:, 8:12], stat[:, 4:8], ACT.Ln)
            act.wait_ge(scalar_tile, count("scalar_tile", "end", 0, 1))
            tile(stat[:, 12:16], stat[:, 8:12], ACT.Exp, scale=-0.5)
            act.wait_ge(vector_tile, count("vector_tile", "end", 0, 2))
            for t in (1, 3):
                tile(ytok[:, t, :], ytok[:, t, :], ACT.Copy, scale=stat[:, t:t + 1])

        @block.vector
        def _(dve):
            where = {}

            def enter(stage, i=0):
                if where:
                    leave()
                where.update(stage=stage, i=i, steps=0)

            def leave():
                want = RAISED["vector_step"].get(where["stage"], 0)
                assert where["steps"] == want, (where, want)

            def step(ins):
                where["steps"] += 1
                ins.then_inc(vector_step, 1)
                dve.wait_ge(vector_step, count("vector_step", where["stage"], where["i"],
                                               where["steps"]))

            def split_lo(stage, i, j):
                n, s = unit(stage, i, j)
                dve.wait_ge(w_hi, n + 1)
                nc.vector.tensor_tensor(wlo[:, s, :], raw[:, s, :], whi[:, s, :].bitcast(F32),
                                        ALU.subtract).then_inc(w_lo, 1)

            def operand_lo(stage, i, k, hi, lo, src, scale=None, bank=None):
                dve.wait_ge(op_hi, count("op_hi", stage, i, k))
                if scale is None:
                    ins = nc.vector.tensor_tensor(lo, src, hi.bitcast(F32), ALU.subtract)
                else:
                    ins = nc.vector.scalar_tensor_tensor(out=lo, in0=src, scalar=scale,
                                                         in1=hi.bitcast(F32), op0=ALU.mult,
                                                         op1=ALU.subtract)
                ins.then_inc(op_lo if bank is None else free[bank], 1)

            def newton(rstd, var, tmp, out):
                step(nc.vector.tensor_tensor(tmp, var, rstd, ALU.mult))
                step(nc.vector.tensor_tensor(tmp, tmp, rstd, ALU.mult))
                step(nc.vector.tensor_scalar(tmp, tmp, -0.5, 1.5, ALU.mult, ALU.add))
                return nc.vector.tensor_tensor(out, tmp, rstd, ALU.mult)

            enter("norm")
            dve.wait_ge(consts, 8)
            step(nc.vector.tensor_copy(recip16[:], steps16[:]))
            step(nc.vector.reciprocal(recip16[:], recip16[:]))
            for g, w in enumerate(POOL_WINDOWS):
                step(nc.vector.tensor_scalar(inv16[:, g, :], recip16[:], 1.0 / w, None, ALU.max))
            step(nc.vector.memset(cum[:, 0:PAD], 0.0))
            wait_full(dve, 7, "norm", 0, 1)
            nc.vector.tensor_copy(vecs[:], banks[7][:, 0:N_VECS]).then_inc(free[7], 1)
            wait_free(dve, 7, "norm", 0, 1)
            dve.wait_ge(scalar_tile, count("scalar_tile", "norm", 0, 4))
            nc.vector.tensor_scalar(stat[:, 4:8], stat[:, 0:4], 1.0 / D, EPS, ALU.mult, ALU.add
                                    ).then_inc(vector_tile, 1)
            dve.wait_ge(vector_tile, count("vector_tile", "norm", 0, 1))
            dve.wait_ge(scalar_tile, count("scalar_tile", "norm", 0, 6))
            step(newton(stat[:, 12:16], stat[:, 4:8], stat[:, 8:12], stat[:, 0:4]))
            for t in range(TB):
                nc.vector.tensor_scalar(big_y[:, t * D:(t + 1) * D], big_x[:, t * D:(t + 1) * D],
                                        stat[:, t:t + 1], None, ALU.mult
                                        ).then_inc(vector_tile, 1)
            split_lo("front", 0, 0)
            for k in range(DB):
                operand_lo("norm", 0, k + 1, op(H_HI + k * S), op(H_LO + k * S), banks[k][:],
                           vecs[:, V_ATTN + k:V_ATTN + k + 1], k)
                if k == 3:
                    split_lo("front", 0, 1)
            split_lo("front", 0, 2)

            enter("front")
            split_lo("front", 0, 3)
            wait_unit(dve, "front", 0, 0)
            nc.vector.tensor_scalar(fz, banks[0][0:H, :], bias_f[:, 0:1], None, ALU.add
                                    ).then_inc(free[0], 1)
            wait_free(dve, 0, "front", 0, 1)
            nc.vector.scalar_tensor_tensor(out=fe, in0=fz, scalar=-1.0, in1=fz, op0=ALU.mult,
                                           op1=ALU.max).then_inc(vector_tile, 1)

            def pool_diff(g, j, bank, k):
                w = POOL_WINDOWS[g]
                wait_unit(dve, "front", 0, j)
                step(nc.vector.tensor_tensor_scan(cum[:, PAD:], ones[:], banks[bank][:], 0.0,
                                                  ALU.mult, ALU.add))
                step(nc.vector.tensor_tensor(diff, cum[:, PAD:], cum[:, PAD - w:PAD + S - w],
                                             ALU.subtract))
                step(nc.vector.tensor_tensor(edge[:], diff[:, 0:PAD], inv16[:, g, :], ALU.mult))
                step(nc.vector.scalar_tensor_tensor(out=diff, in0=diff, scalar=1.0 / w,
                                                    in1=banks[bank][:], op0=ALU.mult,
                                                    op1=ALU.subtract))
                nc.vector.tensor_tensor(diff[:, 0:PAD], edge[:], banks[bank][:, 0:PAD],
                                        ALU.subtract).then_inc(free[bank], 1)

            def diff_lo(k):
                operand_lo("front", 0, k, op(DF_HI), op(DF_LO), diff)

            def pool_lo(g, k):
                operand_lo("front", 0, k, op(BR[1][0] + g * S), op(BR[1][1] + g * S), banks[3][:],
                           vecs[:, V_SCALE + g:V_SCALE + g + 1], 3)

            split_lo("front", 0, 4)
            pool_diff(0, 1, 1, 1)
            diff_lo(1)
            dve.wait_ge(pool_w_hi, 1)
            nc.vector.tensor_tensor(op(PW_LO), pw_raw, op(PW_HI).bitcast(F32), ALU.subtract
                                    ).then_inc(pool_w_lo, 1)
            dve.wait_ge(scalar_tile, count("scalar_tile", "front", 0, 2))
            step(nc.vector.scalar_tensor_tensor(out=fz, in0=fz, scalar=0.0, in1=fe, op0=ALU.min,
                                                op1=ALU.subtract))
            step(nc.vector.tensor_tensor_scan(fF, ones[0:H, :], fz, 0.0, ALU.mult, ALU.add))
            step(nc.vector.tensor_copy(op(F_HI, S, slice(0, H)), fF))
            nc.vector.tensor_tensor(op(F_LO, S, slice(0, H)), fF,
                                    op(F_HI, S, slice(0, H)).bitcast(F32), ALU.subtract
                                    ).then_inc(vector_tile, 1)
            split_lo("front", 0, 5)
            pool_diff(1, 2, 2, 1)
            pool_lo(0, 2)
            diff_lo(3)
            split_lo("front", 0, 6)
            pool_diff(2, 3, 0, 2)
            pool_lo(1, 4)
            diff_lo(5)
            split_lo("front", 0, 7)
            pool_diff(3, 4, 1, 2)
            pool_lo(2, 6)
            diff_lo(7)
            wait_full(dve, 3, "front", 0, 4)
            nc.vector.tensor_copy(f_rows[:].rearrange("p t h -> p (t h)"), banks[3][:, 0:TB * H]
                                  ).then_inc(free[3], 1)
            pool_lo(3, 8)

            with dve.Fori(0, WB) as i:
                enter("pair", i)
                split_lo("pair", i, 3)
                operand_lo("pair", i, 1, op(Q_HI), op(Q_LO), banks[0][:], SCALE, 0)
                split_lo("pair", i, 4)
                operand_lo("pair", i, 2, op(K_HI), op(K_LO), banks[1][:], None, 1)
                for b in range(3, 8):
                    wait_free(dve, b, "front", 0, RAISED[f"free{b}"]["front"])
                for a in range(2):
                    lg = big_y[:, a * L_COLS:(a + 1) * L_COLS]
                    for b in range(TB):
                        n = (b + 1) * P
                        wait_full(dve, 3 + b, "pair", i, a + 1)
                        nc.vector.scalar_tensor_tensor(
                            out=lg[:, L_AT[b]:L_AT[b] + n],
                            in0=big_x[:, bass.ds(i * (2 * S) + a * S, n)],
                            scalar=f_rows[:, b, bass.ds(i * 2 + a, 1)],
                            in1=banks[3 + b][:, 0:n], op0=ALU.add, op1=ALU.add
                            ).then_inc(free[3 + b], 1)
                    for b in range(TB):
                        wait_free(dve, 3 + b, "pair", i, a + 1)
                    diag = lg.rearrange("p (a c) -> p a c", c=P)[:, 0:13:4, :]
                    step(nc.vector.tensor_tensor(
                        diag, diag, mask[:].rearrange("p (a c) -> p a c", a=1)
                        .to_broadcast([P, TB, P]), ALU.add))
                    for b in range(TB):
                        step(nc.vector.tensor_reduce(
                            stat[:, 32 + 4 * a + b:33 + 4 * a + b],
                            lg[:, L_AT[b]:L_AT[b] + (b + 1) * P], AX_X, ALU.max))
                    nc.vector.tensor_scalar(stat[:, 16 + 4 * a:20 + 4 * a],
                                            stat[:, 32 + 4 * a:36 + 4 * a], -1.0, None, ALU.mult
                                            ).then_inc(row_max, 1)
                for a in range(2):
                    dve.wait_ge(exp_done, count("exp_done", "pair", i, a + 1))
                    step(nc.vector.reciprocal(stat[:, 40 + 4 * a:44 + 4 * a],
                                              stat[:, 24 + 4 * a:28 + 4 * a]))
                    for b in range(TB):
                        at = a * L_COLS + L_AT[b]
                        lg = big_y[:, at:at + (b + 1) * P]
                        ins = nc.vector.tensor_scalar(lg, lg, stat[:, 40 + 4 * a + b:41 + 4 * a + b],
                                                      None, ALU.mult)
                    ins.then_inc(probs, 1)
                split_lo("pair", i, 5)
                split_lo("pair", i, 6)
                operand_lo("pair", i, 3, op(V_HI), op(V_LO), banks[7][:], None, 7)
                split_lo("pair", i, 7)
                for a in range(2):
                    for j in range(TB):
                        operand_lo("pair", i, 4 + 4 * a + j,
                                   op(PT[a][0] + PT_AT[j], S - j * P),
                                   op(PT[a][1] + PT_AT[j], S - j * P),
                                   banks[3 + j][:, j * P:S], None, 3 + j)
                split_lo("pair", i, 8)
                wait_unit(dve, "pair", i, 5)
                wait_free(dve, 0, "pair", i, 2)
                nc.vector.tensor_tensor(wk(CV), banks[2][:], wk(CV), ALU.mult
                                        ).then_inc(free[2], 1)
                wait_free(dve, 2, "pair", i, 2)
                for a, b in ((0, 7), (1, 3)):
                    rows = slice(a * HD, (a + 1) * HD)
                    operand_lo("pair", i, 12 + a, operands[rows, bass.ds(BR[0][0] + i * S, S)],
                               operands[rows, bass.ds(BR[0][1] + i * S, S)], banks[b][rows, :],
                               None, b)

                def tap(k):
                    return vecs[:, bass.ds(i + (V_CONV + k * WB), 1)]

                dve.wait_ge(op_lo, count("op_lo", "pair", i, 0))
                step(nc.vector.tensor_scalar(wk(CY), wk(CV), tap(2), None, ALU.mult))
                for k in (1, 0):
                    lag = 2 - k
                    step(nc.vector.scalar_tensor_tensor(
                        out=wk(CY)[:, lag:S], in0=wk(CV)[:, 0:S - lag], scalar=tap(k),
                        in1=wk(CY)[:, lag:S], op0=ALU.mult, op1=ALU.add))
                wait_free(dve, 1, "pair", i, 2)
                nc.vector.tensor_tensor(wk(CY), wk(CY), wk(CB), ALU.mult
                                        ).then_inc(vector_tile, 1)
                operand_lo("pair", i, 14, opd(BR[2][0], i), opd(BR[2][1], i), wk(CY))

            with dve.Fori(0, DB // 2) as i:
                enter("mix", i)

                def gated(dst, j, b, k, br, mm):
                    wait_unit(dve, "mix", i, j)
                    wait_free(dve, br, "mix", i, 1 + mm)
                    nc.vector.tensor_tensor(dst, banks[b][:], wk(GA + br), ALU.mult
                                            ).then_inc(free[b], 1)
                    return lambda: wait_free(dve, b, "mix", i, k)

                for mm in range(2):
                    split_lo("mix", i, 3 + 5 * mm)
                    split_lo("mix", i, 4 + 5 * mm)
                    split_lo("mix", i, 5 + 5 * mm)
                    dve.wait_ge(op_lo, count("op_lo", "mix", i, mm))
                    first = gated(wk(ACC), 2 + 5 * mm, 3, 1 + mm, 0, mm)
                    second = gated(wk(TMP), 2 + 5 * mm, 4, 1 + mm, 1, mm)
                    first()
                    second()
                    step(nc.vector.tensor_tensor(wk(ACC), wk(ACC), wk(TMP), ALU.add))
                    split_lo("mix", i, 6 + 5 * mm)
                    if mm == 0:
                        split_lo("mix", i, 7)
                    gated(wk(TMP), 4, 5 + mm, 1, 2, mm)()
                    nc.vector.tensor_tensor(wk(ACC), wk(ACC), wk(TMP), ALU.add
                                            ).then_inc(vector_tile, 1)
                    operand_lo("mix", i, 1 + mm, opd(MX_HI, i * 2 + mm), opd(MX_LO, i * 2 + mm),
                               wk(ACC))

            def out_block(stage, i, j, m):
                split_lo(stage, i, j + 3)
                wait_unit(dve, stage, i, j)
                wait_free(dve, 3 + j, stage, i, 1)
                x1 = big_x[:, bass.ds(m * S, S)]
                nc.vector.tensor_tensor(x1, banks[j][:], wk(XT), ALU.add).then_inc(free[j], 1)
                wait_free(dve, j, stage, i, 1)
                operand_lo(stage, i, j + 1, opd(H_HI, m), opd(H_LO, m), x1,
                           vecs[:, bass.ds(m + V_FFN, 1)])
                dve.wait_ge(scalar_tile, count("scalar_tile", stage, i, j + 1))
                nc.vector.tensor_tensor(SUMSQ, SUMSQ, wk(SQ), ALU.add).then_inc(sumsq_done, 1)
                dve.wait_ge(sumsq_done, count("sumsq_done", stage, i, j + 1) + 1)

            enter("out")
            nc.vector.memset(SUMSQ, 0.0).then_inc(sumsq_done, 1)
            dve.wait_ge(sumsq_done, 1)
            with dve.Fori(0, 2) as i:
                enter("out", i)
                for j in range(3):
                    out_block("out", i, j, i * 3 + j)
            enter("out_end")
            for j in range(2):
                out_block("out_end", 0, j, 6 + j)

            enter("ffn_first")
            split_lo("ffn_first", 0, 3)
            wait_full(dve, 6, "ffn_first", 0, 1)
            nc.vector.tensor_scalar(VAR, banks[6][:], 1.0 / D, EPS, ALU.mult, ALU.add
                                    ).then_inc(free[6], 1)
            wait_free(dve, 6, "ffn_first", 0, 1)
            dve.wait_ge(scalar_tile, count("scalar_tile", "ffn_first", 0, 2))
            step(newton(RSTD, VAR, SUMSQ, RSTD))

            def hidden(stage, i, j, a):
                if stage == "ffn":
                    split_lo(stage, i, 2 * j + 3)
                wait_unit(dve, stage, i, 2 * j)
                nc.vector.tensor_tensor(wk(A1), banks[a][:], RSTD, ALU.mult).then_inc(free[a], 1)
                split_lo(stage, i, 2 * j + 4)
                wait_unit(dve, stage, i, 2 * j + 1)
                nc.vector.tensor_tensor(wk(B1), banks[a + 1][:], RSTD, ALU.mult
                                        ).then_inc(free[a + 1], 1)
                wait_free(dve, a, stage, i, 1)
                dve.wait_ge(scalar_tile, count("scalar_tile", stage, i,
                                               j + 1 if stage == "ffn" else 3))
                dve.wait_ge(op_lo, count("op_lo", stage, i, j))
                step(nc.vector.tensor_tensor(wk(HD_), wk(A1), wk(SG), ALU.mult))
                wait_free(dve, a + 1, stage, i, 1)
                nc.vector.tensor_tensor(wk(HD_), wk(HD_), wk(B1), ALU.mult
                                        ).then_inc(vector_tile, 1)
                hb = i * 3 + (1 + j) if stage == "ffn" else 0
                operand_lo(stage, i, j + 1, opd(HID_HI, hb), opd(HID_LO, hb), wk(HD_))

            hidden("ffn_first", 0, 0, 0)
            with dve.Fori(0, 7) as i:
                enter("ffn", i)
                for j in range(3):
                    hidden("ffn", i, j, (2 * j + 2) % 6)

            def x2_block(stage, i, mm, m):
                wait_unit(dve, stage, i, 3 * mm + 2)
                nc.vector.tensor_tensor(wk(X2 + mm), banks[2 + mm][:],
                                        big_x[:, bass.ds(m * S, S)], ALU.add
                                        ).then_inc(free[2 + mm], 1)

            def y_block(stage, i, mm, m):
                dve.wait_ge(scalar_tile, count("scalar_tile", stage, i, mm + 1))
                nc.vector.tensor_tensor(
                    ytok[:, :, bass.ds(m * P, P)],
                    banks[6 + mm][:].rearrange("p (t c) -> p t c", c=P),
                    final_g[:, bass.ds(m * P, P)].rearrange("p (a c) -> p a c", a=1)
                    .to_broadcast([P, TB, P]), ALU.mult).then_inc(free[6 + mm], 1)

            dve.wait_ge(final_g_in, 16)
            with dve.Fori(0, 3) as i:
                enter("down", i)
                for j in (3, 4, 5):
                    split_lo("down", i, j)
                x2_block("down", i, 0, i * 2)
                split_lo("down", i, 6)
                y_block("down", i, 0, i * 2)
                split_lo("down", i, 7)
                split_lo("down", i, 8)
                x2_block("down", i, 1, i * 2 + 1)
                y_block("down", i, 1, i * 2 + 1)
            enter("down_end")
            for j in (3, 4, 5):
                split_lo("down_end", 0, j)
            x2_block("down_end", 0, 0, 6)
            y_block("down_end", 0, 0, 6)
            x2_block("down_end", 0, 1, 7)
            y_block("down_end", 0, 1, 7)

            enter("end")
            for b in (6, 7):
                wait_free(dve, b, "down_end", 0, 1)
            step(nc.vector.tensor_reduce(stat[:, 0:4], stat[:, 16:16 + TB * DB].rearrange(
                "p (t m) -> p t m", m=DB), AX_X, ALU.add))
            nc.vector.tensor_scalar(stat[:, 4:8], stat[:, 0:4], 1.0 / D, EPS, ALU.mult, ALU.add
                                    ).then_inc(vector_tile, 1)
            dve.wait_ge(vector_tile, count("vector_tile", "end", 0, 1))
            dve.wait_ge(scalar_tile, count("scalar_tile", "end", 0, 2))
            newton(stat[:, 12:16], stat[:, 4:8], stat[:, 8:12], stat[:, 0:4]
                   ).then_inc(vector_tile, 1)
            dve.wait_ge(vector_tile, count("vector_tile", "end", 0, 2))
            for t in (0, 2):
                nc.vector.tensor_scalar(ytok[:, t, :], ytok[:, t, :], stat[:, t:t + 1], None,
                                        ALU.mult).then_inc(vector_tile, 1)
            leave()


_INS = ["x", "attn_norm", "w_in", "b_forget", "b_gate", "w_proj_attn", "pool_w", "pool_scale",
        "w_proj_pool", "conv_w", "w_proj_conv", "w_out", "ffn_norm", "w_gate_up", "w_down",
        "final_norm"]


def kernel(**inputs):
    import numpy as _np
    import concourse.bacc as _bacc
    from concourse import mybir as _mybir
    from concourse.bass_utils import run_bass_kernel_spmd as _run

    nc = _bacc.Bacc("TRN2", target_bir_lowering=False, num_devices=1)
    arrays, args = {}, []
    for name in _INS:
        a = _np.ascontiguousarray(inputs[name])
        arrays[f"in_{name}_dram"] = a
        args.append(nc.dram_tensor(f"in_{name}_dram", a.shape, _mybir.dt.from_np(a.dtype),
                                   kind="ExternalInput").ap())
    shape = inputs["x"].shape
    args.append(nc.dram_tensor("out_0_dram", shape, F32, kind="ExternalOutput").ap())
    hybrid_block(nc, *args)
    r = _run(nc, [arrays], core_ids=[0])
    return r.results[0]["out_0_dram"]
```

```python
from contextlib import ExitStack

import concourse.bass as bass
from concourse import mybir

ALU = mybir.AluOpType
ACT = mybir.ActivationFunctionType
F32 = mybir.dt.float32
F32R = mybir.dt.float32r
I32 = mybir.dt.int32
AX_X = mybir.AxisListType.X

P = 128
SLOTS = 3
UB = 8
EPS = 1e-6
NEG_INF = -1e30

STAGES = [("norm", 1, 0), ("front", 1, 5), ("pair", 4, 6), ("mix", 4, 9), ("out", 2, 3),
          ("out_end", 1, 2), ("ffn_first", 1, 2), ("ffn", 7, 6),
          ("down_first", 1, 6), ("down", 2, 6), ("down_end", 1, 6), ("end", 1, 0)]

RAISED = {
    "free0": dict(norm=1, front=2, pair=2, mix=2, out=1, out_end=1, ffn_first=1, ffn=1),
    "free1": dict(norm=1, front=2, pair=2, mix=2, out=1, out_end=1, ffn_first=1, ffn=1),
    "free2": dict(norm=1, front=3, pair=2, mix=2, out=1, ffn=1, down_first=1, down=1, down_end=1),
    "free3": dict(norm=1, front=3, pair=5, mix=2, out=1, out_end=1, ffn=1, down_first=1, down=1,
                  down_end=1),
    "free4": dict(norm=1, front=2, pair=4, mix=2, out=1, out_end=1, ffn=1),
    "free5": dict(norm=1, front=2, pair=4, mix=1, out=1, ffn=1),
    "free6": dict(norm=1, front=2, pair=4, mix=1, ffn_first=1, down_first=1, down=1, down_end=1),
    "free7": dict(norm=2, front=2, pair=2, down=1, down_end=2),
    "full0": dict(norm=1), "full1": dict(norm=1), "full2": dict(norm=1, front=2),
    "full3": dict(norm=1, front=3, pair=5, out=1, out_end=1),
    "full4": dict(norm=1, front=2, pair=4, out=1, out_end=1),
    "full5": dict(norm=1, front=2, pair=4, out=1),
    "full6": dict(norm=1, front=2, pair=4, ffn_first=1, down_first=1, down=1, down_end=1),
    "full7": dict(norm=2, front=2, pair=2, down=1, down_end=2),
    "op_hi": dict(norm=8, front=8, pair=14, mix=2, out=3, out_end=2, ffn_first=1, ffn=3),
    "op_lo": dict(front=4, pair=1, mix=2, out=3, out_end=2, ffn_first=1, ffn=3),
    "scalar_tile": dict(norm=12, front=2, out=3, out_end=2, ffn_first=3, ffn=3, down_first=1,
                        down=2, down_end=3, end=4),
    "vector_tile": dict(norm=8, front=2, pair=1, mix=2, ffn_first=1, ffn=3, end=4),
    "row_max": dict(pair=2), "exp_done": dict(pair=2), "probs": dict(pair=2),
    "sumsq_done": dict(out=3, out_end=2),
    "vector_step": dict(norm=23, front=23, pair=15, mix=2, ffn_first=5, ffn=3, end=4),
}


def stage_of(name):
    first = 0
    for s, times, units in STAGES:
        if s == name:
            return first, units
        first += times * units


def count(what, stage, i, k):
    before = 0
    for s, times, _ in STAGES:
        if s == stage:
            return before + i * RAISED[what].get(s, 0) + k
        before += times * RAISED[what].get(s, 0)


def unit(stage, i, j):
    first, per = stage_of(stage)
    return first + j + i * per, (first + j) % SLOTS


def loads_before(stage, i, j):
    first, per = stage_of(stage)
    return (first + j) // SLOTS + 1 + i * (per // SLOTS)


def hybrid_block(nc, x, attn_norm, w_in, b_forget, b_gate, w_proj_attn, pool_w, pool_scale,
                 w_proj_pool, conv_w, w_proj_conv, w_out, ffn_norm, w_gate_up, w_down,
                 final_norm, out):
    x, out = x[0], out[0]
    S, D = x.shape
    H = b_forget.shape[1]
    AW = w_proj_attn.shape[1]
    HD = AW // H
    FH = w_down.shape[1]
    TB, DB, WB, FB = S // P, D // P, AW // P, FH // P
    POOL_WINDOWS = (2, 4, 8, 16)
    PAD = max(POOL_WINDOWS)
    SCALE = float(HD) ** -0.5
    w_in, w_out, w_gate_up, w_down = w_in[0], w_out[0], w_gate_up[0], w_down[0]
    w_proj = [w_proj_attn[0], w_proj_pool[0], w_proj_conv[0]]
    conv_k = conv_w.shape[1]
    COL_Q, COL_K, COL_V, COL_F = 0, AW, 2 * AW, 3 * AW
    COL_U = COL_F + H
    COL_CV, COL_CB, COL_CC = COL_U + AW, COL_U + 2 * AW, COL_U + 3 * AW
    COL_G = COL_U + 4 * AW

    V_ATTN, V_FFN, V_GATE = 0, DB, 2 * DB
    V_SCALE = V_GATE + 3 * DB
    V_CONV = V_SCALE + WB
    N_VECS = V_CONV + conv_k * WB

    with ExitStack() as ctx:
        def sb(name, shape, dt=F32):
            return ctx.enter_context(nc.sbuf_tensor(name, shape, dt))

        def sem(name):
            return ctx.enter_context(nc.semaphore(name))

        operands = sb("operands", [P, (DB + FB) * 2 * S], F32R)
        raw = sb("raw", [P, SLOTS, UB * P])
        whi = sb("whi", [P, SLOTS, UB * P], F32R)
        wlo = sb("wlo", [P, SLOTS, UB * P], F32R)
        big_x = sb("big_x", [P, DB * S])
        big_y = sb("big_y", [P, DB * S])
        work = sb("work", [P, 3072])
        ident = sb("ident", [P, P])
        mask = sb("mask", [P, P])
        ones = sb("ones", [P, S])
        vecs = sb("vecs", [P, N_VECS])
        inv16 = sb("inv16", [P, 4, PAD])
        steps16 = sb("steps16", [P, PAD], I32)
        recip16 = sb("recip16", [P, PAD])
        edge = sb("edge", [P, PAD])
        f_rows = sb("f_rows", [P, TB, H])
        stat = sb("stat", [P, 64])
        bias_f = sb("bias_f", [H, 1])

        def opnd(at, blocks):
            return at, at + blocks * S

        H_HI, H_LO = opnd(0, DB)
        BR = [opnd(2 * DB * S + 2 * WB * S * b, WB) for b in range(3)]
        T0 = 2 * DB * S + 6 * WB * S
        Q_HI, Q_LO, K_HI, K_LO, V_HI, V_LO = [T0 + S * j for j in range(6)]
        PT_AT = [0, 4 * P, 7 * P, 9 * P]
        PT_COLS = 11 * P
        PT = [(T0 + 6 * S + 2 * PT_COLS * a, T0 + 6 * S + 2 * PT_COLS * a + PT_COLS)
              for a in range(2)]
        F_HI, F_LO, SEL = PT[0][0], PT[0][0] + S, PT[0][0] + 2 * S
        DF = [(PT[0][0] + S * j, PT[0][0] + S * (j + 1)) for j in (4, 6)]
        PW_HI, PW_LO = PT[0][0] + 8 * S, PT[0][0] + 9 * S
        MX_HI, MX_LO = opnd(T0, DB)
        HID_HI, HID_LO = opnd(2 * DB * S, FB)

        SQUARED, RSQRT = (1, 2, 5, 8), (4, 7, 10, 12)
        VARIANCE, H_ROWS = (1, 2, 4, 6), (3, 5, 7, 8)
        POOL_MAP = ((3, 1, 1), (2, 2, 1), (3, 3, 3), (2, 3, 2))

        def op(at, n=S, rows=slice(0, P)):
            return operands[rows, at:at + n]

        def pt_at(j):
            return PT_AT[j] + (P if j == TB - 1 else 0)

        def opd(at, index, n=S):
            return operands[:, bass.ds(at + index * S, n)]

        def wk(slot, n=S, rows=slice(0, P)):
            return work[rows, slot * S:slot * S + n]

        VT, CV, CB, CY = 0, 1, 2, 3
        GA, ACC, TMP = 0, 3, 4
        XT, SQ = 0, 1
        A1, SG, B1, HD_ = 0, 1, 2, 3
        X2, JUNK, FG = 0, 2, 4
        cum = work[:, 0:PAD + S]
        diff = work[:, PAD + S:PAD + 2 * S]
        fz = work[0:H, PAD + 2 * S:PAD + 3 * S]
        fe = work[0:H, PAD + 3 * S:PAD + 4 * S]
        fF = work[0:H, PAD + 4 * S:PAD + 5 * S]
        vec_rows = work[0:N_VECS, PAD + 5 * S:PAD + 5 * S + P]
        pw_raw = big_y[:, 0:4 * P]
        L_AT = [0, 3 * P, 6 * P, 9 * P]
        L_COLS = 13 * P
        SUMSQ, VAR, RSTD = [big_y[:, j * S:(j + 1) * S] for j in range(3)]
        XS = [big_y[:, j * S:(j + 1) * S] for j in range(3, 6)]
        ytok = big_y[:].rearrange("p (t d) -> p t d", t=TB)
        final_g = work[:, FG * S:FG * S + D]

        banks = [ctx.enter_context(nc.psum_tensor(f"bank{b}", [P, S], F32)) for b in range(8)]

        x_in = [sem(f"x_in{t}") for t in range(TB)]
        const_in = sem("const_in")
        pool_w_in = sem("pool_w_in")
        xs_in = [sem(f"xs_in{j}") for j in range(3)]
        final_g_in = sem("final_g_in")
        landed = [sem(f"landed{s}") for s in range(SLOTS)]
        loads_begun = sem("loads_begun")
        w_hi = sem("w_hi")
        w_lo = sem("w_lo")
        used = sem("used")
        full = [sem(f"full{b}") for b in range(8)]
        free = [sem(f"free{b}") for b in range(8)]
        sumsq_done = sem("sumsq_done")
        op_hi, op_lo = sem("op_hi"), sem("op_lo")
        scalar_tile, vector_tile = sem("scalar_tile"), sem("vector_tile")
        row_max, exp_done, probs = sem("row_max"), sem("exp_done"), sem("probs")
        vector_step = sem("vector_step")
        consts = sem("consts")
        pool_w_hi, pool_w_lo = sem("pool_w_hi"), sem("pool_w_lo")
        stored = sem("stored")

        def wait_full(eng, b, stage, i, k):
            eng.wait_ge(full[b], count(f"full{b}", stage, i, k))

        def wait_unit(eng, stage, i, j):
            eng.wait_ge(used, unit(stage, i, j)[0] + 1)

        def wait_free(eng, b, stage, i, k):
            eng.wait_ge(free[b], count(f"free{b}", stage, i, k))

        block = ctx.enter_context(nc.Block())

        @block.sync
        def _(sp):
            def load(stage, i, j, halves):
                n, s = unit(stage, i, j)
                if not (stage == "front" and n < SLOTS):
                    sp.wait_ge(w_lo, n - SLOTS + 1)
                    sp.sem_inc(loads_begun, 1)
                for src, at in halves:
                    nb = src.shape[0] // P
                    dst = raw[:, s, at * P:(at + nb) * P].rearrange("p (k c) -> p k c", c=P)
                    sp.dma_start(dst, src.rearrange("(k p) c -> p k c", p=P)
                                 ).then_inc(landed[s], 16)

            def columns(w, col, rows=0, nb=8):
                h = (nb + 1) // 2 if nb != 6 else 4
                c = bass.ds(col, P)
                return [(w[rows:rows + h * P, c], 0), (w[rows + h * P:rows + nb * P, c], h)]

            def load_x(t):
                sp.dma_start(big_x[:, t * D:(t + 1) * D], x[t * P:(t + 1) * P, :]
                             ).then_inc(x_in[t], 16)

            load_x(0)
            load_x(1)
            for src, at in ((attn_norm, V_ATTN), (ffn_norm, V_FFN), (b_gate, V_GATE),
                            (pool_scale, V_SCALE)):
                r = src[0].rearrange("(r c) -> r c", c=P)
                sp.dma_start(vec_rows[at:at + r.shape[0], :], r).then_inc(const_in, 16)
            sp.dma_start(vec_rows[V_CONV:N_VECS, :],
                         conv_w[0].rearrange("k (r c) -> (k r) c", c=P)).then_inc(const_in, 16)
            sp.dma_start(bias_f[:], b_forget[0].rearrange("(h a) -> h a", a=1)
                         ).then_inc(const_in, 16)
            for t in range(2, TB):
                load_x(t)

            front = [COL_F] + [COL_U + g * P for g in range(4)]
            for j in range(3):
                load("front", 0, j, columns(w_in, front[j]))
            sp.wait_ge(full[DB - 2], count(f"full{DB - 2}", "norm", 0, 1))
            sp.wait_ge(full[DB - 1], count(f"full{DB - 1}", "norm", 0, 2))
            sp.dma_start(pw_raw.rearrange("p (g d) -> p g d", g=4),
                         pool_w[0].rearrange("g c d -> c g d")).then_inc(pool_w_in, 16)
            for j in range(3, 5):
                load("front", 0, j, columns(w_in, front[j]))
            with sp.Fori(0, WB) as i:
                for j, col in enumerate((COL_Q, COL_K, COL_V, COL_CV, COL_CB, COL_CC)):
                    load("pair", i, j, columns(w_in, i * P + col))

            with sp.Fori(0, DB // 2) as i:
                def gate(j, br, mm):
                    load("mix", i, j, columns(w_in, i * (2 * P) + (COL_G + br * D + mm * P)))

                def proj(j, first, second):
                    load("mix", i, j,
                         [(w_proj[br][:, bass.ds(i * (2 * P) + mm * P, P)], at)
                          for (br, mm), at in ((first, 0), (second, WB))])

                gate(0, 0, 0)
                gate(1, 1, 0)
                proj(2, (0, 0), (1, 0))
                gate(3, 2, 0)
                proj(4, (2, 0), (2, 1))
                gate(5, 0, 1)
                gate(6, 1, 1)
                proj(7, (0, 1), (1, 1))
                gate(8, 2, 1)

            def out_loads(stage, i, m0, nm):
                for j in range(nm):
                    load(stage, i, j, columns(w_out, m0(i, j)))
                for j in range(nm):
                    if stage == "out":
                        sp.wait_ge(full[3], count("full3", "pair", 3, 4))
                        sp.wait_ge(full[3 + j], count(f"full{3 + j}", "out", i, 0))
                    else:
                        sp.wait_ge(full[3 + j], count(f"full{3 + j}", "out", 1, 1))
                    sp.sem_inc(loads_begun, 1)
                    sp.dma_start(XS[j].rearrange("p (t c) -> p t c", c=P),
                                 x.rearrange("(t p) c -> p t c", p=P)[:, :, bass.ds(m0(i, j), P)]
                                 ).then_inc(xs_in[j], 16)

            with sp.Fori(0, 2) as i:
                out_loads("out", i, lambda i, j: i * (3 * P) + j * P, 3)
            out_loads("out_end", 0, lambda i, j: (6 + j) * P, 2)

            load("ffn_first", 0, 0, columns(w_gate_up, 0))
            load("ffn_first", 0, 1, columns(w_gate_up, FH))
            with sp.Fori(0, 7) as i:
                for j in range(3):
                    load("ffn", i, 2 * j, columns(w_gate_up, i * (3 * P) + (1 + j) * P))
                    load("ffn", i, 2 * j + 1, columns(w_gate_up, i * (3 * P) + (1 + j) * P + FH))

            sp.wait_ge(sumsq_done, DB + 1)
            sp.dma_start(final_g, final_norm.rearrange("(a d) -> a d", a=1).to_broadcast([P, D])
                         ).then_inc(final_g_in, 16)

            def down_loads(stage, i, col):
                for mm in range(2):
                    for c in range(3):
                        nb = 8 if c < 2 else FB - 16
                        load(stage, i, 3 * mm + c, columns(w_down, col + mm * P, c * 8 * P, nb))

            down_loads("down_first", 0, 0)
            with sp.Fori(0, 2) as i:
                down_loads("down", i, i * (2 * P) + 2 * P)
            down_loads("down_end", 0, 6 * P)

            for t in range(TB):
                if t % 2 == 0:
                    sp.wait_ge(vector_tile, count("vector_tile", "end", 0, 3 + t // 2))
                else:
                    sp.wait_ge(scalar_tile, count("scalar_tile", "end", 0, 3 + t // 2))
                sp.dma_start(out[t * P:(t + 1) * P, :], ytok[:, t, :]).then_inc(stored, 16)
            sp.wait_ge(stored, 16 * TB)

        @block.gpsimd
        def _(pool):
            nc.gpsimd.memset(ident[:], 0.0).then_inc(consts, 1)
            nc.gpsimd.memset(mask[:], 0.0).then_inc(consts, 1)
            nc.gpsimd.memset(op(SEL, H * P, slice(0, H)).bitcast(F32), 0.0).then_inc(consts, 1)
            nc.gpsimd.memset(ones[:], 1.0).then_inc(consts, 1)
            pool.wait_ge(consts, 4)
            nc.gpsimd.affine_select(out=ident[:], in_=ident[:], compare_op=ALU.not_equal, fill=1.0,
                                    base=0, pattern=[[-1, P]], channel_multiplier=1
                                    ).then_inc(consts, 1)
            nc.gpsimd.affine_select(out=mask[:], in_=mask[:], compare_op=ALU.is_ge, fill=NEG_INF,
                                    base=0, pattern=[[-1, P]], channel_multiplier=1
                                    ).then_inc(consts, 1)
            sel = op(SEL, H * P, slice(0, H)).rearrange("p (h c) -> p h c", h=H)
            nc.gpsimd.affine_select(out=sel, in_=sel.bitcast(F32), compare_op=ALU.not_equal,
                                    fill=-1.0, base=0, pattern=[[-1, H], [0, P]],
                                    channel_multiplier=1).then_inc(consts, 1)
            nc.gpsimd.iota(steps16[:], pattern=[[1, PAD]], base=1, channel_multiplier=0
                           ).then_inc(consts, 1)

        @block.tensor
        def _(pe):
            def begin(b, stage, i, k):
                before = count(f"free{b}", stage, i, k - 1)
                if not (isinstance(before, int) and before == 0):
                    pe.wait_ge(free[b], before)

            def product(b, s, blocks, hi, lo, first, last, width=S, ready=None):
                for n, (wb, k) in enumerate(blocks):
                    if ready is not None:
                        ready(k)
                    w = slice(wb * P, (wb + 1) * P)
                    a, z = first and n == 0, last and n == len(blocks) - 1
                    nc.tensor.matmul(banks[b][:, 0:width], whi[:, s, w], op(hi + k * S),
                                     start=a, stop=False)
                    nc.tensor.matmul(banks[b][:, 0:width], whi[:, s, w], op(lo + k * S),
                                     start=False, stop=False)
                    mm = nc.tensor.matmul(banks[b][:, 0:width], wlo[:, s, w], op(hi + k * S),
                                          start=False, stop=z)
                return mm

            def unit_ready(stage, i, j):
                n, s = unit(stage, i, j)
                pe.wait_ge(w_lo, n + 1)
                return s

            def whole(b, stage, i, j, k, hi, lo, ready=None):
                s = unit_ready(stage, i, j)
                begin(b, stage, i, k)
                mm = product(b, s, [(c, c) for c in range(UB)], hi, lo, True, True, ready=ready)
                mm.then_inc(used, 1)

            pe.wait_ge(const_in, 16 * 6)
            pe.wait_ge(consts, 8)
            nc.tensor.transpose(banks[7][:, 0:N_VECS], vec_rows, ident[0:N_VECS, 0:N_VECS]
                                ).then_inc(full[7], 1)
            for t in range(TB):
                pe.wait_ge(vector_tile, count("vector_tile", "norm", 0, H_ROWS[t]))
                for k in range(DB):
                    if t == 0 and k == 7:
                        begin(7, "norm", 0, 2)
                    tr = nc.tensor.transpose(banks[k][:, t * P:(t + 1) * P],
                                             big_y[:, t * D + k * P:t * D + (k + 1) * P], ident[:])
                    if t == TB - 1:
                        tr.then_inc(full[k], 1)

            def h_ready(k):
                wait_free(pe, k, "norm", 0, 1 if k < 7 else 2)

            def pool_map(g):
                pe.wait_ge(op_lo, count("op_lo", "front", 0, g + 1))
                if g == 0:
                    pe.wait_ge(pool_w_lo, 1)
                b, use, _ = POOL_MAP[g]
                begin(b, "front", 0, use)
                w = slice(g * P, (g + 1) * P)
                dh, dl = DF[g % 2]
                nc.tensor.matmul(banks[b][:], op(PW_HI)[:, w], op(dh), start=True, stop=False)
                nc.tensor.matmul(banks[b][:], op(PW_HI)[:, w], op(dl), start=False, stop=False)
                nc.tensor.matmul(banks[b][:], op(PW_LO)[:, w], op(dh), start=False, stop=True
                                 ).then_inc(full[b], 1)

            whole(0, "front", 0, 0, 1, H_HI, H_LO, h_ready)
            whole(1, "front", 0, 1, 1, H_HI, H_LO)
            whole(2, "front", 0, 2, 1, H_HI, H_LO)
            pool_map(0)
            whole(0, "front", 0, 3, 2, H_HI, H_LO)
            pool_map(1)
            whole(1, "front", 0, 4, 2, H_HI, H_LO)
            pe.wait_ge(vector_tile, count("vector_tile", "front", 0, 2))

            def spread_f(heads):
                for h in heads:
                    b = 4 + h % 4
                    begin(b, "front", 0, h // 4 + 1)
                    sel = op(SEL + h * P, P, slice(0, H))
                    nc.tensor.matmul(banks[b][:], sel, op(F_HI, S, slice(0, H)),
                                     start=True, stop=False)
                    nc.tensor.matmul(banks[b][:], sel, op(F_LO, S, slice(0, H)),
                                     start=False, stop=True).then_inc(full[b], 1)

            spread_f(range(4))
            begin(3, "front", 0, 2)
            for t in range(TB):
                tr = nc.tensor.transpose(banks[3][:, t * H:(t + 1) * H], fF[:, t * P:(t + 1) * P],
                                         ident[0:H, 0:H])
            tr.then_inc(full[3], 1)
            pool_map(2)
            spread_f(range(4, H))
            pool_map(3)

            with pe.Fori(0, WB) as i:
                whole(0, "pair", i, 0, 1, H_HI, H_LO)
                whole(1, "pair", i, 1, 1, H_HI, H_LO)
                s = unit_ready("pair", i, 2)
                begin(2, "pair", i, 1)
                product(2, s, [(c, c) for c in range(3)], H_HI, H_LO, True, False)
                wait_free(pe, 0, "pair", i, 1)
                wait_free(pe, 1, "pair", i, 1)
                for a in range(2):
                    rows = slice(a * HD, (a + 1) * HD)
                    for b in range(TB):
                        begin(3 + b, "pair", i, a + 1)
                        n = max(b + 1, 2) * P
                        dst = banks[3 + b][:, 0:n]
                        nc.tensor.matmul(dst, op(Q_HI + b * P, P, rows), op(K_HI, n, rows),
                                         start=True, stop=False)
                        nc.tensor.matmul(dst, op(Q_HI + b * P, P, rows), op(K_LO, n, rows),
                                         start=False, stop=False)
                        nc.tensor.matmul(dst, op(Q_LO + b * P, P, rows), op(K_HI, n, rows),
                                         start=False, stop=True).then_inc(full[3 + b], 1)
                product(2, s, [(c, c) for c in range(3, 8)], H_HI, H_LO, False, True
                        ).then_inc(used, 1)
                whole(0, "pair", i, 3, 2, H_HI, H_LO)
                wait_free(pe, 2, "pair", i, 1)
                begin(7, "pair", i, 1)
                for t in range(TB):
                    tr = nc.tensor.transpose(banks[7][:, t * P:(t + 1) * P],
                                             wk(VT)[:, t * P:(t + 1) * P], ident[:])
                tr.then_inc(full[7], 1)
                whole(1, "pair", i, 4, 2, H_HI, H_LO)

                def turn_probs(a):
                    pe.wait_ge(probs, count("probs", "pair", i, a + 1))
                    for j in range(TB):
                        begin(3 + j, "pair", i, 3 + a)
                        for b in range(j, TB):
                            at = a * L_COLS + L_AT[b] + j * P
                            tr = nc.tensor.transpose(banks[3 + j][:, b * P:(b + 1) * P],
                                                     big_y[:, at:at + P], ident[:])
                        tr.then_inc(full[3 + j], 1)

                turn_probs(0)
                s = unit_ready("pair", i, 5)
                begin(2, "pair", i, 2)
                product(2, s, [(c, c) for c in range(4)], H_HI, H_LO, True, False)
                turn_probs(1)
                product(2, s, [(c, c) for c in range(4, 8)], H_HI, H_LO, False, True
                        ).then_inc(used, 1)

                for a, b, k in ((0, 7, 2), (1, 3, 5)):
                    wait_free(pe, 7, "pair", i, 1)
                    for j in range(TB):
                        wait_free(pe, 3 + j, "pair", i, 3 + a)
                    begin(b, "pair", i, k)
                    for j in range(TB):
                        first = min(j, TB - 2)
                        dst = banks[b][:, first * P:S]
                        n, at = S - first * P, PT_AT[j]
                        vj = slice(j * P, (j + 1) * P)
                        nc.tensor.matmul(dst, op(V_HI)[:, vj], op(PT[a][0] + at, n),
                                         start=(j == 0), stop=False)
                        nc.tensor.matmul(dst, op(V_HI)[:, vj], op(PT[a][1] + at, n),
                                         start=False, stop=False)
                        mm = nc.tensor.matmul(dst, op(V_LO)[:, vj], op(PT[a][0] + at, n),
                                              start=False, stop=(j == TB - 1))
                    mm.then_inc(full[b], 1)

            with pe.Fori(0, DB // 2) as i:
                def project(j, parts):
                    s = unit_ready("mix", i, j)
                    for half, (br, b, k) in enumerate(parts):
                        begin(b, "mix", i, k)
                        mm = product(b, s, [(half * WB + c, c) for c in range(WB)], *BR[br],
                                     True, True)
                    mm.then_inc(used, 1)

                whole(0, "mix", i, 0, 1, H_HI, H_LO)
                whole(1, "mix", i, 1, 1, H_HI, H_LO)
                wait_free(pe, 7, "pair", 3, 2)
                wait_free(pe, 3, "pair", 3, 5)
                project(2, [(0, 3, 1), (1, 4, 1)])
                whole(2, "mix", i, 3, 1, H_HI, H_LO)
                pe.wait_ge(op_lo, count("op_lo", "pair", 3, 1))
                project(4, [(2, 5, 1), (2, 6, 1)])
                whole(0, "mix", i, 5, 2, H_HI, H_LO)
                whole(1, "mix", i, 6, 2, H_HI, H_LO)
                project(7, [(0, 3, 2), (1, 4, 2)])
                whole(2, "mix", i, 8, 2, H_HI, H_LO)

            def out_block(stage, i, j, loads):
                pe.wait_ge(xs_in[j], loads)
                begin(3 + j, stage, i, 1)
                for t in range(TB):
                    tr = nc.tensor.transpose(banks[3 + j][:, t * P:(t + 1) * P],
                                             XS[j][:, t * P:(t + 1) * P], ident[:])
                tr.then_inc(full[3 + j], 1)

                def merged(k):
                    if k == DB - 1:
                        pe.wait_ge(op_lo, count("op_lo", "mix", 3, 2))
                    elif k == 0:
                        pe.wait_ge(op_lo, count("op_lo", "mix", 3, 1))

                whole(j, stage, i, j, 1, MX_HI, MX_LO, merged)

            with pe.Fori(0, 2) as i:
                for j in range(3):
                    out_block("out", i, j, i * 16 + 16)
            for j in range(2):
                out_block("out_end", 0, j, 48)

            def x1_ready(k):
                if k < 6:
                    pe.wait_ge(op_lo, count("op_lo", "out", 1, 3))
                else:
                    pe.wait_ge(op_lo, count("op_lo", "out_end", 0, k - 5))

            whole(0, "ffn_first", 0, 0, 1, H_HI, H_LO, x1_ready)
            pe.wait_ge(sumsq_done, DB + 1)
            begin(6, "ffn_first", 0, 1)
            nc.tensor.matmul(banks[6][:], ones[:, 0:P], SUMSQ, start=True, stop=True
                             ).then_inc(full[6], 1)
            whole(1, "ffn_first", 0, 1, 1, H_HI, H_LO)
            with pe.Fori(0, 7) as i:
                for j in range(3):
                    a = (2 * j + 2) % 6
                    whole(a, "ffn", i, 2 * j, 1, H_HI, H_LO)
                    whole(a + 1, "ffn", i, 2 * j + 1, 1, H_HI, H_LO)

            def down_pair(stage, i):
                def part(b, j, c):
                    s = unit_ready(stage, i, j)
                    nb = 8 if c < 2 else FB - 16
                    if c == 0:
                        begin(b, stage, i, 1)

                    def hidden(k):
                        if k == FB - 1:
                            pe.wait_ge(op_lo, count("op_lo", "ffn", 6, 3))

                    mm = product(b, s, [(q, c * 8 + q) for q in range(nb)], HID_HI, HID_LO,
                                 c == 0, c == 2, ready=hidden if stage == "down_first" else None)
                    mm.then_inc(used, 1)

                def turn(mm, before, k):
                    wait_free(pe, 2 + mm, stage, i, before)
                    begin(6 + mm, stage, i, k)
                    for t in range(TB):
                        tr = nc.tensor.transpose(banks[6 + mm][:, t * P:(t + 1) * P],
                                                 wk(X2 + mm)[:, t * P:(t + 1) * P], ident[:])
                    tr.then_inc(full[6 + mm], 1)

                part(2, 0, 0)
                if stage != "down_first":
                    turn(1, 0, 1)
                part(2, 1, 1)
                part(2, 2, 2)
                part(3, 3, 0)
                turn(0, 1, 1)
                part(3, 4, 1)
                part(3, 5, 2)
                if stage == "down_end":
                    turn(1, 1, 2)

            pe.wait_ge(op_lo, count("op_lo", "ffn", 6, 2))
            down_pair("down_first", 0)
            with pe.Fori(0, 2) as i:
                down_pair("down", i)
            down_pair("down_end", 0)

        @block.scalar
        def _(act):
            def split_hi(stage, i, j):
                n, s = unit(stage, i, j)
                act.wait_ge(landed[s], 32 * loads_before(stage, i, j))
                if not (stage == "front" and n < SLOTS):
                    act.wait_ge(used, n - SLOTS + 1)
                nc.scalar.copy(whi[:, s, :], raw[:, s, :]).then_inc(w_hi, 1)

            def operand_hi(dst, src, scale=1.0):
                nc.scalar.activation(dst, src, ACT.Copy, scale=scale).then_inc(op_hi, 1)

            def tile(dst, src, func, **kw):
                return nc.scalar.activation(dst, src, func, **kw).then_inc(scalar_tile, 1)

            nc.scalar.preload_act_table_set("natural_log_exp_and_others")
            def square(t):
                act.wait_ge(x_in[t], 16)
                tile(big_y[:, t * D:(t + 1) * D], big_x[:, t * D:(t + 1) * D], ACT.Square,
                     accum_out=stat[:, t:t + 1])

            square(0)
            for t in range(TB):
                if t + 1 < TB:
                    square(t + 1)
                act.wait_ge(vector_tile, count("vector_tile", "norm", 0, VARIANCE[t]))
                tile(stat[:, 8 + t:9 + t], stat[:, 4 + t:5 + t], ACT.Ln)
                act.wait_ge(scalar_tile, count("scalar_tile", "norm", 0, RSQRT[t] - 1))
                tile(stat[:, 12 + t:13 + t], stat[:, 8 + t:9 + t], ACT.Exp, scale=-0.5)
            split_hi("front", 0, 0)
            split_hi("front", 0, 1)
            wait_free(act, 7, "norm", 0, 1)
            for k in range(DB):
                wait_full(act, k, "norm", 0, 1 if k < 7 else 2)
                operand_hi(op(H_HI + k * S), banks[k][:], vecs[:, V_ATTN + k:V_ATTN + k + 1])
            split_hi("front", 0, 2)
            act.wait_ge(vector_tile, count("vector_tile", "front", 0, 1))
            tile(fe, fe, ACT.Exp, scale=-1.0)
            act.wait_ge(scalar_tile, count("scalar_tile", "front", 0, 1))
            tile(fe, fe, ACT.Ln, bias=1.0)
            split_hi("front", 0, 3)
            act.wait_ge(pool_w_in, 16)
            nc.scalar.copy(op(PW_HI), pw_raw).then_inc(pool_w_hi, 1)

            def pool_out(g):
                b, _, filled = POOL_MAP[g]
                wait_full(act, b, "front", 0, filled)
                operand_hi(op(BR[1][0] + g * S), banks[b][:], vecs[:, V_SCALE + g:V_SCALE + g + 1])

            def diff_hi(g):
                if g >= 2:
                    b, _, filled = POOL_MAP[g - 2]
                    wait_full(act, b, "front", 0, filled)
                wait_free(act, (1, 2, 0, 1)[g], "front", 0, (1, 1, 2, 2)[g])
                operand_hi(op(DF[g % 2][0]), diff)

            def copy_f(heads):
                for h in heads:
                    b = 4 + h % 4
                    wait_full(act, b, "front", 0, h // 4 + 1)
                    nc.scalar.copy(big_x[:, h * S:(h + 1) * S], banks[b][:]).then_inc(free[b], 1)

            diff_hi(0)
            split_hi("front", 0, 4)
            pool_out(0)
            diff_hi(1)
            split_hi("front", 0, 5)
            pool_out(1)
            diff_hi(2)
            split_hi("front", 0, 6)
            copy_f(range(4))
            diff_hi(3)
            pool_out(2)
            copy_f(range(4, H))
            split_hi("front", 0, 7)
            pool_out(3)

            with act.Fori(0, WB) as i:
                wait_unit(act, "pair", i, 0)
                operand_hi(op(Q_HI), banks[0][:], SCALE)
                split_hi("pair", i, 3)
                wait_unit(act, "pair", i, 1)
                operand_hi(op(K_HI), banks[1][:])
                split_hi("pair", i, 4)
                for a in range(2):
                    act.wait_ge(row_max, count("row_max", "pair", i, a + 1))
                    for b in range(TB):
                        lg = big_y[:, a * L_COLS + L_AT[b]:a * L_COLS + L_AT[b] + (b + 1) * P]
                        at = 4 * a + b
                        e = nc.scalar.activation(lg, lg, ACT.Exp, bias=stat[:, 16 + at:17 + at],
                                                 accum_out=stat[:, 24 + at:25 + at])
                    e.then_inc(exp_done, 1)
                    if a == 0:
                        wait_unit(act, "pair", i, 2)
                        nc.scalar.copy(wk(VT), banks[2][:]).then_inc(free[2], 1)
                        split_hi("pair", i, 5)
                wait_unit(act, "pair", i, 3)
                nc.scalar.copy(wk(CV), banks[0][:]).then_inc(free[0], 1)
                wait_full(act, 7, "pair", i, 1)
                operand_hi(op(V_HI), banks[7][:])
                split_hi("pair", i, 6)
                wait_unit(act, "pair", i, 4)
                nc.scalar.copy(wk(CB), banks[1][:]).then_inc(free[1], 1)
                split_hi("pair", i, 7)
                for a in range(2):
                    for j in range(TB):
                        wait_full(act, 3 + j, "pair", i, 3 + a)
                        operand_hi(op(PT[a][0] + pt_at(j), S - j * P), banks[3 + j][:, j * P:S])
                for a, b, k in ((0, 7, 2), (1, 3, 5)):
                    rows = slice(a * HD, (a + 1) * HD)
                    wait_full(act, b, "pair", i, k)
                    operand_hi(operands[rows, bass.ds(BR[0][0] + i * S, S)], banks[b][rows, :])
                act.wait_ge(vector_tile, count("vector_tile", "pair", i, 1))
                operand_hi(opd(BR[2][0], i), wk(CY))
                split_hi("pair", i, 8)

            nc.scalar.preload_act_table(ACT.Sigmoid)
            with act.Fori(0, DB // 2) as i:
                def gate(j, b, k, br, mm):
                    wait_unit(act, "mix", i, j)
                    if mm == 0:
                        wait_free(act, (3, 4, 6)[br], "mix", i, 0)
                    else:
                        wait_free(act, (3, 4, 5)[br], "mix", i, 1)
                    nc.scalar.activation(wk(GA + br), banks[b][:], ACT.Sigmoid,
                                         bias=vecs[:, bass.ds(i * 2 + (V_GATE + br * DB + mm), 1)]
                                         ).then_inc(free[b], 1)

                def merged_hi(mm):
                    act.wait_ge(vector_tile, count("vector_tile", "mix", i, mm + 1))
                    operand_hi(opd(MX_HI, i * 2 + mm), wk(ACC))

                gate(0, 0, 1, 0, 0)
                split_hi("mix", i, 3)
                gate(1, 1, 1, 1, 0)
                split_hi("mix", i, 4)
                split_hi("mix", i, 5)
                gate(3, 2, 1, 2, 0)
                split_hi("mix", i, 6)
                merged_hi(0)
                split_hi("mix", i, 7)
                gate(5, 0, 2, 0, 1)
                split_hi("mix", i, 8)
                gate(6, 1, 2, 1, 1)
                split_hi("mix", i, 9)
                split_hi("mix", i, 10)
                gate(8, 2, 2, 2, 1)
                merged_hi(1)
                split_hi("mix", i, 11)

            def out_block(stage, i, j, m, nm):
                wait_full(act, 3 + j, stage, i, 1)
                nc.scalar.copy(wk(XT), banks[3 + j][:]).then_inc(free[3 + j], 1)
                act.wait_ge(sumsq_done, count("sumsq_done", stage, i, j) + 1)
                wait_free(act, j, stage, i, 1)
                x1 = big_x[:, bass.ds(m * S, S)]
                operand_hi(opd(H_HI, m), x1, vecs[:, bass.ds(m + V_FFN, 1)])
                tile(wk(SQ), x1, ACT.Square)
                split_hi(stage, i, j + 3)

            with act.Fori(0, 2) as i:
                for j in range(3):
                    out_block("out", i, j, i * 3 + j, 3)
            for j in range(2):
                out_block("out_end", 0, j, 6 + j, 2)

            def hidden(stage, i, j, a):
                wait_free(act, a, stage, i, 1)
                tile(wk(SG), wk(A1), ACT.Sigmoid)
                split_hi(stage, i, 2 * j + 3)
                act.wait_ge(vector_tile, count("vector_tile", stage, i, j + 1))
                hb = i * 3 + (1 + j) if stage == "ffn" else 0
                operand_hi(opd(HID_HI, hb), wk(HD_))
                split_hi(stage, i, 2 * j + 4)

            nc.scalar.preload_act_table_set("natural_log_exp_and_others")
            wait_free(act, 6, "ffn_first", 0, 1)
            tile(RSTD, VAR, ACT.Ln)
            act.wait_ge(scalar_tile, count("scalar_tile", "ffn_first", 0, 1))
            tile(RSTD, RSTD, ACT.Exp, scale=-0.5)
            nc.scalar.preload_act_table(ACT.Sigmoid)
            hidden("ffn_first", 0, 0, 0)
            with act.Fori(0, 7) as i:
                for j in range(3):
                    hidden("ffn", i, j, (2 * j + 2) % 6)

            def squares(stage, i, mm, m, k):
                wait_full(act, 6 + mm, stage, i, k)
                for t in range(TB):
                    sq = nc.scalar.activation(wk(JUNK)[:, t * P:(t + 1) * P],
                                              banks[6 + mm][:, t * P:(t + 1) * P], ACT.Square,
                                              accum_out=stat[:, bass.ds(m + (16 + t * DB), 1)])
                sq.then_inc(scalar_tile, 1)

            def down_pair(stage, i, m):
                split_hi(stage, i, 3)
                if stage != "down_first":
                    squares(stage, i, 1, m + -1, 1)
                split_hi(stage, i, 4)
                split_hi(stage, i, 5)
                if stage != "down_end":
                    split_hi(stage, i, 6)
                squares(stage, i, 0, m, 1)
                if stage != "down_end":
                    split_hi(stage, i, 7)
                    split_hi(stage, i, 8)
                else:
                    squares(stage, i, 1, m + 1, 2)

            nc.scalar.preload_act_table_set("natural_log_exp_and_others")
            down_pair("down_first", 0, 0)
            with act.Fori(0, 2) as i:
                down_pair("down", i, i * 2 + 2)
            down_pair("down_end", 0, 6)

            act.wait_ge(vector_tile, count("vector_tile", "end", 0, 1))
            tile(stat[:, 8:12], stat[:, 4:8], ACT.Ln)
            act.wait_ge(scalar_tile, count("scalar_tile", "end", 0, 1))
            tile(stat[:, 12:16], stat[:, 8:12], ACT.Exp, scale=-0.5)
            act.wait_ge(vector_tile, count("vector_tile", "end", 0, 2))
            wait_free(act, 7, "down_end", 0, 2)
            for t in (1, 3):
                tile(ytok[:, t, :], ytok[:, t, :], ACT.Copy, scale=stat[:, t:t + 1])

        @block.vector
        def _(dve):
            where = {}

            def enter(stage, i=0):
                if where:
                    leave()
                where.update(stage=stage, i=i, steps=0)

            def leave():
                want = RAISED["vector_step"].get(where["stage"], 0)
                assert where["steps"] == want, (where, want)

            def step(ins):
                where["steps"] += 1
                ins.then_inc(vector_step, 1)
                dve.wait_ge(vector_step, count("vector_step", where["stage"], where["i"],
                                               where["steps"]))

            def split_lo(stage, i, j):
                n, s = unit(stage, i, j)
                dve.wait_ge(w_hi, n + 1)
                nc.vector.tensor_tensor(wlo[:, s, :], raw[:, s, :], whi[:, s, :].bitcast(F32),
                                        ALU.subtract).then_inc(w_lo, 1)

            def operand_lo(stage, i, k, hi, lo, src, scale=None, bank=None):
                dve.wait_ge(op_hi, count("op_hi", stage, i, k))
                if scale is None:
                    ins = nc.vector.tensor_tensor(lo, src, hi.bitcast(F32), ALU.subtract)
                else:
                    ins = nc.vector.scalar_tensor_tensor(out=lo, in0=src, scalar=scale,
                                                         in1=hi.bitcast(F32), op0=ALU.mult,
                                                         op1=ALU.subtract)
                ins.then_inc(op_lo if bank is None else free[bank], 1)

            def newton(rstd, var, tmp, out):
                step(nc.vector.tensor_tensor(tmp, var, rstd, ALU.mult))
                step(nc.vector.tensor_tensor(tmp, tmp, rstd, ALU.mult))
                step(nc.vector.tensor_scalar(tmp, tmp, -0.5, 1.5, ALU.mult, ALU.add))
                return nc.vector.tensor_tensor(out, tmp, rstd, ALU.mult)

            enter("norm")
            dve.wait_ge(consts, 8)
            step(nc.vector.tensor_copy(recip16[:], steps16[:]))
            step(nc.vector.reciprocal(recip16[:], recip16[:]))
            for g, w in enumerate(POOL_WINDOWS):
                step(nc.vector.tensor_scalar(inv16[:, g, :], recip16[:], 1.0 / w, None, ALU.max))
            step(nc.vector.memset(cum[:, 0:PAD], 0.0))
            def mean_square(t):
                dve.wait_ge(scalar_tile, count("scalar_tile", "norm", 0, SQUARED[t]))
                nc.vector.tensor_scalar(stat[:, 4 + t:5 + t], stat[:, t:t + 1], 1.0 / D, EPS,
                                        ALU.mult, ALU.add).then_inc(vector_tile, 1)

            mean_square(0)
            for t in range(TB):
                if t + 1 < TB:
                    mean_square(t + 1)
                if t == 1:
                    wait_full(dve, 7, "norm", 0, 1)
                    nc.vector.tensor_copy(vecs[:], banks[7][:, 0:N_VECS]).then_inc(free[7], 1)
                    wait_free(dve, 7, "norm", 0, 1)
                ss, var, tmp, rstd = [stat[:, c + t:c + t + 1] for c in (0, 4, 8, 12)]
                dve.wait_ge(vector_tile, count("vector_tile", "norm", 0, VARIANCE[t]))
                dve.wait_ge(scalar_tile, count("scalar_tile", "norm", 0, RSQRT[t]))
                step(newton(rstd, var, tmp, ss))
                nc.vector.tensor_scalar(big_y[:, t * D:(t + 1) * D], big_x[:, t * D:(t + 1) * D],
                                        ss, None, ALU.mult).then_inc(vector_tile, 1)
            split_lo("front", 0, 0)
            split_lo("front", 0, 1)
            for k in range(DB):
                operand_lo("norm", 0, k + 1, op(H_HI + k * S), op(H_LO + k * S), banks[k][:],
                           vecs[:, V_ATTN + k:V_ATTN + k + 1], k)
            split_lo("front", 0, 2)

            enter("front")
            wait_unit(dve, "front", 0, 0)
            nc.vector.tensor_scalar(fz, banks[0][0:H, :], bias_f[:, 0:1], None, ALU.add
                                    ).then_inc(free[0], 1)
            wait_free(dve, 0, "front", 0, 1)
            nc.vector.scalar_tensor_tensor(out=fe, in0=fz, scalar=-1.0, in1=fz, op0=ALU.mult,
                                           op1=ALU.max).then_inc(vector_tile, 1)

            def pool_diff(g, j, bank, k):
                w = POOL_WINDOWS[g]
                wait_unit(dve, "front", 0, j)
                step(nc.vector.tensor_tensor_scan(cum[:, PAD:], ones[:], banks[bank][:], 0.0,
                                                  ALU.mult, ALU.add))
                step(nc.vector.tensor_tensor(diff, cum[:, PAD:], cum[:, PAD - w:PAD + S - w],
                                             ALU.subtract))
                step(nc.vector.tensor_tensor(edge[:], diff[:, 0:PAD], inv16[:, g, :], ALU.mult))
                step(nc.vector.scalar_tensor_tensor(out=diff, in0=diff, scalar=1.0 / w,
                                                    in1=banks[bank][:], op0=ALU.mult,
                                                    op1=ALU.subtract))
                nc.vector.tensor_tensor(diff[:, 0:PAD], edge[:], banks[bank][:, 0:PAD],
                                        ALU.subtract).then_inc(free[bank], 1)

            def diff_lo(g, k):
                operand_lo("front", 0, k, op(DF[g % 2][0]), op(DF[g % 2][1]), diff)

            def pool_lo(g, k):
                b = POOL_MAP[g][0]
                operand_lo("front", 0, k, op(BR[1][0] + g * S), op(BR[1][1] + g * S), banks[b][:],
                           vecs[:, V_SCALE + g:V_SCALE + g + 1], b)

            dve.wait_ge(scalar_tile, count("scalar_tile", "front", 0, 2))
            step(nc.vector.scalar_tensor_tensor(out=fz, in0=fz, scalar=0.0, in1=fe, op0=ALU.min,
                                                op1=ALU.subtract))
            step(nc.vector.tensor_tensor_scan(fF, ones[0:H, :], fz, 0.0, ALU.mult, ALU.add))
            step(nc.vector.tensor_copy(op(F_HI, S, slice(0, H)), fF))
            nc.vector.tensor_tensor(op(F_LO, S, slice(0, H)), fF,
                                    op(F_HI, S, slice(0, H)).bitcast(F32), ALU.subtract
                                    ).then_inc(vector_tile, 1)
            pool_diff(0, 1, 1, 1)
            split_lo("front", 0, 3)
            diff_lo(0, 1)
            dve.wait_ge(pool_w_hi, 1)
            nc.vector.tensor_tensor(op(PW_LO), pw_raw, op(PW_HI).bitcast(F32), ALU.subtract
                                    ).then_inc(pool_w_lo, 1)
            dve.wait_ge(op_lo, 1)
            pool_diff(1, 2, 2, 1)
            split_lo("front", 0, 4)
            pool_lo(0, 2)
            diff_lo(1, 3)
            dve.wait_ge(op_lo, 2)
            pool_diff(2, 3, 0, 2)
            split_lo("front", 0, 5)
            pool_lo(1, 4)
            diff_lo(2, 5)
            dve.wait_ge(op_lo, 3)
            pool_diff(3, 4, 1, 2)
            wait_full(dve, 3, "front", 0, 2)
            nc.vector.tensor_copy(f_rows[:].rearrange("p t h -> p (t h)"), banks[3][:, 0:TB * H]
                                  ).then_inc(free[3], 1)
            diff_lo(3, 6)
            split_lo("front", 0, 6)
            pool_lo(2, 7)
            split_lo("front", 0, 7)
            pool_lo(3, 8)
            for b in range(4, 8):
                wait_full(dve, b, "front", 0, 2)
            for a in range(2):
                for half in PT[a]:
                    zeros = op(half + PT_AT[TB - 1], P).bitcast(F32)
                    step(nc.vector.memset(zeros, 0.0))

            with dve.Fori(0, WB) as i:
                enter("pair", i)
                operand_lo("pair", i, 1, op(Q_HI), op(Q_LO), banks[0][:], SCALE, 0)
                split_lo("pair", i, 3)
                operand_lo("pair", i, 2, op(K_HI), op(K_LO), banks[1][:], None, 1)
                split_lo("pair", i, 4)
                for b in range(3, 8):
                    wait_free(dve, b, "front", 0, RAISED[f"free{b}"]["front"])
                for a in range(2):
                    lg = big_y[:, a * L_COLS:(a + 1) * L_COLS]
                    for b in range(TB):
                        n = (b + 1) * P
                        wait_full(dve, 3 + b, "pair", i, a + 1)
                        nc.vector.scalar_tensor_tensor(
                            out=lg[:, L_AT[b]:L_AT[b] + n],
                            in0=big_x[:, bass.ds(i * (2 * S) + a * S, n)],
                            scalar=f_rows[:, b, bass.ds(i * 2 + a, 1)],
                            in1=banks[3 + b][:, 0:n], op0=ALU.add, op1=ALU.add
                            ).then_inc(free[3 + b], 1)
                    for b in range(TB):
                        wait_free(dve, 3 + b, "pair", i, a + 1)
                    diag = lg.rearrange("p (a c) -> p a c", c=P)[:, 0:13:4, :]
                    step(nc.vector.tensor_tensor(
                        diag, diag, mask[:].rearrange("p (a c) -> p a c", a=1)
                        .to_broadcast([P, TB, P]), ALU.add))
                    for b in range(TB):
                        step(nc.vector.tensor_reduce(
                            stat[:, 32 + 4 * a + b:33 + 4 * a + b],
                            lg[:, L_AT[b]:L_AT[b] + (b + 1) * P], AX_X, ALU.max))
                    nc.vector.tensor_scalar(stat[:, 16 + 4 * a:20 + 4 * a],
                                            stat[:, 32 + 4 * a:36 + 4 * a], -1.0, None, ALU.mult
                                            ).then_inc(row_max, 1)
                for a in range(2):
                    dve.wait_ge(exp_done, count("exp_done", "pair", i, a + 1))
                    step(nc.vector.reciprocal(stat[:, 40 + 4 * a:44 + 4 * a],
                                              stat[:, 24 + 4 * a:28 + 4 * a]))
                    for b in range(TB):
                        at = a * L_COLS + L_AT[b]
                        lg = big_y[:, at:at + (b + 1) * P]
                        ins = nc.vector.tensor_scalar(lg, lg, stat[:, 40 + 4 * a + b:41 + 4 * a + b],
                                                      None, ALU.mult)
                    ins.then_inc(probs, 1)
                split_lo("pair", i, 5)
                operand_lo("pair", i, 3, op(V_HI), op(V_LO), banks[7][:], None, 7)
                split_lo("pair", i, 6)
                split_lo("pair", i, 7)
                for a in range(2):
                    for j in range(TB):
                        operand_lo("pair", i, 4 + 4 * a + j,
                                   op(PT[a][0] + pt_at(j), S - j * P),
                                   op(PT[a][1] + pt_at(j), S - j * P),
                                   banks[3 + j][:, j * P:S], None, 3 + j)
                wait_unit(dve, "pair", i, 5)
                wait_free(dve, 0, "pair", i, 2)
                nc.vector.tensor_tensor(wk(CV), banks[2][:], wk(CV), ALU.mult
                                        ).then_inc(free[2], 1)
                wait_free(dve, 2, "pair", i, 2)
                for a, b in ((0, 7), (1, 3)):
                    rows = slice(a * HD, (a + 1) * HD)
                    operand_lo("pair", i, 12 + a, operands[rows, bass.ds(BR[0][0] + i * S, S)],
                               operands[rows, bass.ds(BR[0][1] + i * S, S)], banks[b][rows, :],
                               None, b)

                def tap(k):
                    return vecs[:, bass.ds(i + (V_CONV + k * WB), 1)]

                dve.wait_ge(op_lo, count("op_lo", "pair", i, 0))
                step(nc.vector.tensor_scalar(wk(CY), wk(CV), tap(2), None, ALU.mult))
                for k in (1, 0):
                    lag = 2 - k
                    step(nc.vector.scalar_tensor_tensor(
                        out=wk(CY)[:, lag:S], in0=wk(CV)[:, 0:S - lag], scalar=tap(k),
                        in1=wk(CY)[:, lag:S], op0=ALU.mult, op1=ALU.add))
                wait_free(dve, 1, "pair", i, 2)
                nc.vector.tensor_tensor(wk(CY), wk(CY), wk(CB), ALU.mult
                                        ).then_inc(vector_tile, 1)
                operand_lo("pair", i, 14, opd(BR[2][0], i), opd(BR[2][1], i), wk(CY))
                split_lo("pair", i, 8)

            with dve.Fori(0, DB // 2) as i:
                enter("mix", i)

                def gated(dst, j, b, k, br, mm):
                    wait_unit(dve, "mix", i, j)
                    wait_free(dve, br, "mix", i, 1 + mm)
                    nc.vector.tensor_tensor(dst, banks[b][:], wk(GA + br), ALU.mult
                                            ).then_inc(free[b], 1)
                    return lambda: wait_free(dve, b, "mix", i, k)

                for mm in range(2):
                    split_lo("mix", i, 3 + 5 * mm)
                    split_lo("mix", i, 4 + 5 * mm)
                    dve.wait_ge(op_lo, count("op_lo", "mix", i, mm))
                    first = gated(wk(ACC), 2 + 5 * mm, 3, 1 + mm, 0, mm)
                    second = gated(wk(TMP), 2 + 5 * mm, 4, 1 + mm, 1, mm)
                    first()
                    second()
                    step(nc.vector.tensor_tensor(wk(ACC), wk(ACC), wk(TMP), ALU.add))
                    split_lo("mix", i, 5 + 5 * mm)
                    if mm == 0:
                        split_lo("mix", i, 6)
                    gated(wk(TMP), 4, 5 + mm, 1, 2, mm)()
                    nc.vector.tensor_tensor(wk(ACC), wk(ACC), wk(TMP), ALU.add
                                            ).then_inc(vector_tile, 1)
                    operand_lo("mix", i, 1 + mm, opd(MX_HI, i * 2 + mm), opd(MX_LO, i * 2 + mm),
                               wk(ACC))
                    split_lo("mix", i, 7 if mm == 0 else 11)

            def out_block(stage, i, j, m):
                wait_unit(dve, stage, i, j)
                wait_free(dve, 3 + j, stage, i, 1)
                x1 = big_x[:, bass.ds(m * S, S)]
                nc.vector.tensor_tensor(x1, banks[j][:], wk(XT), ALU.add).then_inc(free[j], 1)
                wait_free(dve, j, stage, i, 1)
                operand_lo(stage, i, j + 1, opd(H_HI, m), opd(H_LO, m), x1,
                           vecs[:, bass.ds(m + V_FFN, 1)])
                dve.wait_ge(scalar_tile, count("scalar_tile", stage, i, j + 1))
                nc.vector.tensor_tensor(SUMSQ, SUMSQ, wk(SQ), ALU.add).then_inc(sumsq_done, 1)
                dve.wait_ge(sumsq_done, count("sumsq_done", stage, i, j + 1) + 1)
                split_lo(stage, i, j + 3)

            enter("out")
            nc.vector.memset(SUMSQ, 0.0).then_inc(sumsq_done, 1)
            dve.wait_ge(sumsq_done, 1)
            with dve.Fori(0, 2) as i:
                enter("out", i)
                for j in range(3):
                    out_block("out", i, j, i * 3 + j)
            enter("out_end")
            for j in range(2):
                out_block("out_end", 0, j, 6 + j)

            enter("ffn_first")
            wait_full(dve, 6, "ffn_first", 0, 1)
            nc.vector.tensor_scalar(VAR, banks[6][:], 1.0 / D, EPS, ALU.mult, ALU.add
                                    ).then_inc(free[6], 1)
            wait_free(dve, 6, "ffn_first", 0, 1)
            dve.wait_ge(scalar_tile, count("scalar_tile", "ffn_first", 0, 2))
            step(newton(RSTD, VAR, SUMSQ, RSTD))

            def hidden(stage, i, j, a):
                wait_unit(dve, stage, i, 2 * j)
                nc.vector.tensor_tensor(wk(A1), banks[a][:], RSTD, ALU.mult).then_inc(free[a], 1)
                split_lo(stage, i, 2 * j + 3)
                wait_unit(dve, stage, i, 2 * j + 1)
                nc.vector.tensor_tensor(wk(B1), banks[a + 1][:], RSTD, ALU.mult
                                        ).then_inc(free[a + 1], 1)
                wait_free(dve, a, stage, i, 1)
                dve.wait_ge(scalar_tile, count("scalar_tile", stage, i,
                                               j + 1 if stage == "ffn" else 3))
                dve.wait_ge(op_lo, count("op_lo", stage, i, j))
                step(nc.vector.tensor_tensor(wk(HD_), wk(A1), wk(SG), ALU.mult))
                wait_free(dve, a + 1, stage, i, 1)
                nc.vector.tensor_tensor(wk(HD_), wk(HD_), wk(B1), ALU.mult
                                        ).then_inc(vector_tile, 1)
                hb = i * 3 + (1 + j) if stage == "ffn" else 0
                operand_lo(stage, i, j + 1, opd(HID_HI, hb), opd(HID_LO, hb), wk(HD_))
                split_lo(stage, i, 2 * j + 4)

            hidden("ffn_first", 0, 0, 0)
            with dve.Fori(0, 7) as i:
                enter("ffn", i)
                for j in range(3):
                    hidden("ffn", i, j, (2 * j + 2) % 6)

            def x2_block(stage, i, mm, m):
                wait_unit(dve, stage, i, 3 * mm + 2)
                nc.vector.tensor_tensor(wk(X2 + mm), banks[2 + mm][:],
                                        big_x[:, bass.ds(m * S, S)], ALU.add
                                        ).then_inc(free[2 + mm], 1)

            def y_block(stage, i, mm, m, k):
                dve.wait_ge(scalar_tile, count("scalar_tile", stage, i, k))
                nc.vector.tensor_tensor(
                    ytok[:, :, bass.ds(m * P, P)],
                    banks[6 + mm][:].rearrange("p (t c) -> p t c", c=P),
                    final_g[:, bass.ds(m * P, P)].rearrange("p (a c) -> p a c", a=1)
                    .to_broadcast([P, TB, P]), ALU.mult).then_inc(free[6 + mm], 1)

            def down_pair(stage, i, m):
                enter(stage, i)
                before = stage != "down_first"
                split_lo(stage, i, 3)
                if before:
                    y_block(stage, i, 1, m + -1, 1)
                split_lo(stage, i, 4)
                x2_block(stage, i, 0, m)
                split_lo(stage, i, 5)
                if stage != "down_end":
                    split_lo(stage, i, 6)
                y_block(stage, i, 0, m, 1 + before)
                if stage != "down_end":
                    split_lo(stage, i, 7)
                x2_block(stage, i, 1, m + 1)
                if stage != "down_end":
                    split_lo(stage, i, 8)

            dve.wait_ge(final_g_in, 16)
            down_pair("down_first", 0, 0)
            with dve.Fori(0, 2) as i:
                down_pair("down", i, i * 2 + 2)
            down_pair("down_end", 0, 6)

            enter("end")
            dve.wait_ge(scalar_tile, count("scalar_tile", "down_end", 0, 3))
            step(nc.vector.tensor_reduce(stat[:, 0:4], stat[:, 16:16 + TB * DB].rearrange(
                "p (t m) -> p t m", m=DB), AX_X, ALU.add))
            nc.vector.tensor_scalar(stat[:, 4:8], stat[:, 0:4], 1.0 / D, EPS, ALU.mult, ALU.add
                                    ).then_inc(vector_tile, 1)
            y_block("down_end", 0, 1, 7, 3)
            dve.wait_ge(vector_tile, count("vector_tile", "end", 0, 1))
            dve.wait_ge(scalar_tile, count("scalar_tile", "end", 0, 2))
            newton(stat[:, 12:16], stat[:, 4:8], stat[:, 8:12], stat[:, 0:4]
                   ).then_inc(vector_tile, 1)
            dve.wait_ge(vector_tile, count("vector_tile", "end", 0, 2))
            wait_free(dve, 6, "down_end", 0, 1)
            wait_free(dve, 7, "down_end", 0, 2)
            for t in (0, 2):
                nc.vector.tensor_scalar(ytok[:, t, :], ytok[:, t, :], stat[:, t:t + 1], None,
                                        ALU.mult).then_inc(vector_tile, 1)
            leave()


_INS = ["x", "attn_norm", "w_in", "b_forget", "b_gate", "w_proj_attn", "pool_w", "pool_scale",
        "w_proj_pool", "conv_w", "w_proj_conv", "w_out", "ffn_norm", "w_gate_up", "w_down",
        "final_norm"]


def kernel(**inputs):
    import numpy as _np
    import concourse.bacc as _bacc
    from concourse import mybir as _mybir
    from concourse.bass_utils import run_bass_kernel_spmd as _run

    nc = _bacc.Bacc("TRN2", target_bir_lowering=False, num_devices=1)
    arrays, args = {}, []
    for name in _INS:
        a = _np.ascontiguousarray(inputs[name])
        arrays[f"in_{name}_dram"] = a
        args.append(nc.dram_tensor(f"in_{name}_dram", a.shape, _mybir.dt.from_np(a.dtype),
                                   kind="ExternalInput").ap())
    shape = inputs["x"].shape
    args.append(nc.dram_tensor("out_0_dram", shape, F32, kind="ExternalOutput").ap())
    hybrid_block(nc, *args)
    r = _run(nc, [arrays], core_ids=[0])
    return r.results[0]["out_0_dram"]
```

```python
from contextlib import ExitStack

import concourse.bass as bass
from concourse import mybir

ALU = mybir.AluOpType
ACT = mybir.ActivationFunctionType
F32 = mybir.dt.float32
F32R = mybir.dt.float32r
I32 = mybir.dt.int32
AX_X = mybir.AxisListType.X

P = 128
SLOTS = 3
UB = 8
EPS = 1e-6
NEG_INF = -1e30

STAGES = [("norm", 1, 0), ("front", 1, 5), ("pair", 4, 6), ("mix", 4, 9), ("out", 1, 8),
          ("ffn_first", 1, 2), ("ffn", 7, 6), ("down_a", 3, 3), ("down_a_end", 1, 2),
          ("down_b", 3, 3), ("down_b_end", 1, 2)]

RAISED = {
    "free0": dict(norm=1, front=2, pair=2, mix=2, out=2, ffn_first=1, ffn=1, down_b_end=1),
    "free1": dict(norm=1, front=2, pair=2, mix=2, out=2, ffn_first=1, ffn=1, down_b_end=1),
    "free2": dict(norm=1, front=3, pair=2, mix=2, out=2, ffn=1, down_a_end=1),
    "free3": dict(norm=1, front=3, pair=5, mix=2, out=2, ffn=1, down_a_end=1),
    "free4": dict(norm=1, front=2, pair=4, mix=2, out=2, ffn=1, down_b_end=1),
    "free5": dict(norm=1, front=2, pair=4, mix=1, out=2, ffn=1, down_b_end=1),
    "free6": dict(norm=1, front=2, pair=4, mix=1, out=2, ffn_first=1, down_a_end=1),
    "free7": dict(norm=2, front=2, pair=2, out=2, down_a_end=1),
    "full0": dict(norm=1, out=2, down_b_end=1), "full1": dict(norm=1, out=2, down_b_end=1),
    "full2": dict(norm=1, front=2, out=2, down_a_end=1),
    "full3": dict(norm=1, front=3, pair=5, out=1),
    "full4": dict(norm=1, front=2, pair=4, out=2, down_b_end=1),
    "full5": dict(norm=1, front=2, pair=4, out=2, down_b_end=1),
    "full6": dict(norm=1, front=2, pair=4, out=2, ffn_first=1, down_a_end=1),
    "full7": dict(norm=2, front=2, pair=2, out=1, down_a_end=1),
    "op_hi": dict(norm=8, front=8, pair=15, mix=2, out=8, ffn_first=1, ffn=3),
    "op_lo": dict(front=4, pair=1, mix=2, ffn_first=1, ffn=3),
    "scalar_tile": dict(norm=12, front=2, out=8, ffn_first=3, ffn=3, down_a_end=4,
                        down_b_end=16),
    "vector_tile": dict(norm=8, front=2, pair=1, mix=2, ffn_first=3, ffn=3, down_b_end=16),
    "row_max": dict(pair=2), "exp_done": dict(pair=2), "probs": dict(pair=2),
    "vector_step": dict(norm=19, front=23, pair=15, mix=2, ffn_first=6, ffn=3, down_b_end=9),
}


def stage_of(name):
    first = 0
    for s, times, units in STAGES:
        if s == name:
            return first, units
        first += times * units


def count(what, stage, i, k):
    before = 0
    for s, times, _ in STAGES:
        if s == stage:
            return before + i * RAISED[what].get(s, 0) + k
        before += times * RAISED[what].get(s, 0)


def unit(stage, i, j):
    first, per = stage_of(stage)
    return first + j + i * per, (first + j) % SLOTS


def loads_before(stage, i, j):
    first, per = stage_of(stage)
    return (first + j) // SLOTS + 1 + i * (per // SLOTS)


def hybrid_block(nc, x, attn_norm, w_in, b_forget, b_gate, w_proj_attn, pool_w, pool_scale,
                 w_proj_pool, conv_w, w_proj_conv, w_out, ffn_norm, w_gate_up, w_down,
                 final_norm, out):
    x, out = x[0], out[0]
    S, D = x.shape
    H = b_forget.shape[1]
    AW = w_proj_attn.shape[1]
    HD = AW // H
    FH = w_down.shape[1]
    TB, DB, WB, FB = S // P, D // P, AW // P, FH // P
    POOL_WINDOWS = (2, 4, 8, 16)
    PAD = max(POOL_WINDOWS)
    SCALE = float(HD) ** -0.5
    w_in, w_out, w_gate_up, w_down = w_in[0], w_out[0], w_gate_up[0], w_down[0]
    w_proj = [w_proj_attn[0], w_proj_pool[0], w_proj_conv[0]]
    conv_k = conv_w.shape[1]
    COL_Q, COL_K, COL_V, COL_F = 0, AW, 2 * AW, 3 * AW
    COL_U = COL_F + H
    COL_CV, COL_CB, COL_CC = COL_U + AW, COL_U + 2 * AW, COL_U + 3 * AW
    COL_G = COL_U + 4 * AW

    V_ATTN, V_FFN, V_GATE = 0, DB, 2 * DB
    V_SCALE = V_GATE + 3 * DB
    V_CONV = V_SCALE + WB
    N_VECS = V_CONV + conv_k * WB

    with ExitStack() as ctx:
        def sb(name, shape, dt=F32):
            return ctx.enter_context(nc.sbuf_tensor(name, shape, dt))

        def sem(name):
            return ctx.enter_context(nc.semaphore(name))

        operands = sb("operands", [P, (DB + FB) * 2 * S], F32R)
        raw = sb("raw", [P, SLOTS, UB * P])
        whi = sb("whi", [P, SLOTS, UB * P], F32R)
        wlo = sb("wlo", [P, SLOTS, UB * P], F32R)
        big_x = sb("big_x", [P, DB * S])
        big_y = sb("big_y", [P, DB * S])
        work = sb("work", [P, 3072])
        ident = sb("ident", [P, P])
        mask = sb("mask", [P, P])
        ones = sb("ones", [P, S])
        vecs = sb("vecs", [P, N_VECS])
        inv16 = sb("inv16", [P, 4, PAD])
        steps16 = sb("steps16", [P, PAD], I32)
        recip16 = sb("recip16", [P, PAD])
        edge = sb("edge", [P, PAD])
        f_rows = sb("f_rows", [P, TB, H])
        stat = sb("stat", [P, 64])
        bias_f = sb("bias_f", [H, 1])

        def opnd(at, blocks):
            return at, at + blocks * S

        H_HI, H_LO = opnd(0, DB)
        BR = [opnd(2 * DB * S + 2 * WB * S * b, WB) for b in range(3)]
        T0 = 2 * DB * S + 6 * WB * S
        QS, KK = [T0, T0 + S], [T0 + 2 * S, T0 + 3 * S]
        K_LO, V_HI, V_LO = [T0 + S * j for j in (4, 5, 6)]
        PT_AT = [0, 4 * P, 7 * P, 9 * P]
        PT_COLS = 11 * P
        PT = [(T0 + 7 * S + 2 * PT_COLS * a, T0 + 7 * S + 2 * PT_COLS * a + PT_COLS)
              for a in range(2)]
        F_HI, F_LO, SEL = PT[0][0], PT[0][0] + S, PT[0][0] + 2 * S
        DF = [(PT[0][0] + S * j, PT[0][0] + S * (j + 1)) for j in (4, 6)]
        PW_HI, PW_LO = PT[0][0] + 8 * S, PT[0][0] + 9 * S
        MX_HI, MX_LO = opnd(T0, DB)
        HID_HI, HID_LO = opnd(2 * DB * S, FB)

        SQUARED, RSQRT = (1, 2, 5, 8), (4, 7, 10, 12)
        VARIANCE, H_ROWS = (1, 2, 4, 6), (3, 5, 7, 8)
        POOL_MAP = ((3, 1, 1), (2, 2, 1), (3, 3, 3), (2, 3, 2))

        def op(at, n=S, rows=slice(0, P)):
            return operands[rows, at:at + n]

        def half_rows(a):
            return slice(a * HD, (a + 1) * HD)

        def pt_at(j):
            return PT_AT[j] + (P if j == TB - 1 else 0)

        def opd(at, index, n=S):
            return operands[:, bass.ds(at + index * S, n)]

        def wk(slot, n=S, rows=slice(0, P)):
            return work[rows, slot * S:slot * S + n]

        VT, CV, CB, CY = 0, 1, 2, 3
        GA, ACC, TMP = 0, 3, 4
        A1, SG, B1, HD_ = 0, 1, 2, 3
        JUNK_OUT, JUNK, FG = 5, 2, 4
        cum = work[:, 0:PAD + S]
        diff = work[:, PAD + S:PAD + 2 * S]
        fz = work[0:H, PAD + 2 * S:PAD + 3 * S]
        fe = work[0:H, PAD + 3 * S:PAD + 4 * S]
        fF = work[0:H, PAD + 4 * S:PAD + 5 * S]
        vec_rows = work[0:N_VECS, PAD + 5 * S:PAD + 5 * S + P]
        pw_raw = big_y[:, 0:4 * P]
        L_AT = [0, 3 * P, 6 * P, 9 * P]
        L_COLS = 13 * P
        RSTD, DIAG = big_y[:, 0:S], big_y[:, S:2 * S]
        HALF = D // 2
        DOWN_BANKS = ((6, 7, 2, 3), (4, 5, 0, 1))
        TAIL_TILES = [4 * t for t in range(TB)]
        SS_OUT, SS_DOWN = 48, 56

        def tok(buf, t, c):
            return buf[:, t * D + c * HALF:t * D + (c + 1) * HALF]

        final_g = work[:, FG * S:FG * S + D]

        banks = [ctx.enter_context(nc.psum_tensor(f"bank{b}", [P, S], F32)) for b in range(8)]

        x_in = [sem(f"x_in{t}") for t in range(TB)]
        const_in = sem("const_in")
        pool_w_in = sem("pool_w_in")
        x_again = [sem(f"x_again{t}") for t in range(TB)]
        final_g_in = sem("final_g_in")
        landed = [sem(f"landed{s}") for s in range(SLOTS)]
        loads_begun = sem("loads_begun")
        w_hi = sem("w_hi")
        w_lo = sem("w_lo")
        used = sem("used")
        full = [sem(f"full{b}") for b in range(8)]
        free = [sem(f"free{b}") for b in range(8)]
        op_hi, op_lo = sem("op_hi"), sem("op_lo")
        scalar_tile, vector_tile = sem("scalar_tile"), sem("vector_tile")
        row_max, exp_done, probs = sem("row_max"), sem("exp_done"), sem("probs")
        vector_step = sem("vector_step")
        consts = sem("consts")
        pool_w_hi, pool_w_lo = sem("pool_w_hi"), sem("pool_w_lo")
        stored = sem("stored")

        def wait_full(eng, b, stage, i, k):
            eng.wait_ge(full[b], count(f"full{b}", stage, i, k))

        def wait_unit(eng, stage, i, j):
            eng.wait_ge(used, unit(stage, i, j)[0] + 1)

        def wait_free(eng, b, stage, i, k):
            eng.wait_ge(free[b], count(f"free{b}", stage, i, k))

        block = ctx.enter_context(nc.Block())

        @block.sync
        def _(sp):
            def load(stage, i, j, halves, width=P):
                n, s = unit(stage, i, j)
                if not (stage == "front" and n < SLOTS):
                    sp.wait_ge(w_lo, n - SLOTS + 1)
                    sp.sem_inc(loads_begun, 1)
                for src, at in halves:
                    nb = src.shape[0] // P
                    dst = raw[:, s, at * width:(at + nb) * width].rearrange(
                        "p (k c) -> p k c", c=width)
                    sp.dma_start(dst, src.rearrange("(k p) c -> p k c", p=P)
                                 ).then_inc(landed[s], 16)

            def columns(w, col):
                c = bass.ds(col, P)
                return [(w[0:4 * P, c], 0), (w[4 * P:8 * P, c], 4)]

            def load_rows(stage, i, j, w, row, c):
                cols = slice(c * HALF, (c + 1) * HALF)
                load(stage, i, j, [(w[bass.ds(row, P), cols], 0),
                                   (w[bass.ds(row + P, P), cols], 1)], HALF)

            def load_x(t):
                sp.dma_start(big_x[:, t * D:(t + 1) * D], x[t * P:(t + 1) * P, :]
                             ).then_inc(x_in[t], 16)

            load_x(0)
            load_x(1)
            for src, at in ((attn_norm, V_ATTN), (ffn_norm, V_FFN), (b_gate, V_GATE),
                            (pool_scale, V_SCALE)):
                r = src[0].rearrange("(r c) -> r c", c=P)
                sp.dma_start(vec_rows[at:at + r.shape[0], :], r).then_inc(const_in, 16)
            sp.dma_start(vec_rows[V_CONV:N_VECS, :],
                         conv_w[0].rearrange("k (r c) -> (k r) c", c=P)).then_inc(const_in, 16)
            sp.dma_start(bias_f[:], b_forget[0].rearrange("(h a) -> h a", a=1)
                         ).then_inc(const_in, 16)
            for t in range(2, TB):
                load_x(t)

            front = [COL_F] + [COL_U + g * P for g in range(4)]
            for j in range(3):
                load("front", 0, j, columns(w_in, front[j]))
            sp.wait_ge(full[DB - 2], count(f"full{DB - 2}", "norm", 0, 1))
            sp.wait_ge(full[DB - 1], count(f"full{DB - 1}", "norm", 0, 2))
            sp.dma_start(pw_raw.rearrange("p (g d) -> p g d", g=4),
                         pool_w[0].rearrange("g c d -> c g d")).then_inc(pool_w_in, 16)
            for j in range(3, 5):
                load("front", 0, j, columns(w_in, front[j]))
            with sp.Fori(0, WB) as i:
                for j, col in enumerate((COL_Q, COL_K, COL_V, COL_CV, COL_CB, COL_CC)):
                    load("pair", i, j, columns(w_in, i * P + col))

            with sp.Fori(0, DB // 2) as i:
                def gate(j, br, mm):
                    load("mix", i, j, columns(w_in, i * (2 * P) + (COL_G + br * D + mm * P)))

                def proj(j, first, second):
                    load("mix", i, j,
                         [(w_proj[br][:, bass.ds(i * (2 * P) + mm * P, P)], at)
                          for (br, mm), at in ((first, 0), (second, WB))])

                gate(0, 0, 0)
                gate(1, 1, 0)
                proj(2, (0, 0), (1, 0))
                gate(3, 2, 0)
                proj(4, (2, 0), (2, 1))
                gate(5, 0, 1)
                gate(6, 1, 1)
                proj(7, (0, 1), (1, 1))
                gate(8, 2, 1)

            for j in range(8):
                load_rows("out", 0, j, w_out, j % 4 * 2 * P, j // 4)
                if j < TB:
                    if j == 0:
                        for b in range(3, 7):
                            sp.wait_ge(full[b], count(f"full{b}", "pair", 3, 4))
                        sp.sem_inc(loads_begun, 1)
                    sp.dma_start(big_y[:, j * D:(j + 1) * D], x[j * P:(j + 1) * P, :]
                                 ).then_inc(x_again[j], 16)

            load("ffn_first", 0, 0, columns(w_gate_up, 0))
            load("ffn_first", 0, 1, columns(w_gate_up, FH))
            with sp.Fori(0, 7) as i:
                for j in range(3):
                    load("ffn", i, 2 * j, columns(w_gate_up, i * (3 * P) + (1 + j) * P))
                    load("ffn", i, 2 * j + 1, columns(w_gate_up, i * (3 * P) + (1 + j) * P + FH))

            sp.wait_ge(scalar_tile, count("scalar_tile", "out", 0, 8))
            sp.dma_start(final_g, final_norm.rearrange("(a d) -> a d", a=1).to_broadcast([P, D])
                         ).then_inc(final_g_in, 16)

            for c, part in enumerate("ab"):
                with sp.Fori(0, 3) as i:
                    for j in range(3):
                        load_rows(f"down_{part}", i, j, w_down, i * (6 * P) + 2 * j * P, c)
                for j in range(2):
                    load_rows(f"down_{part}_end", 0, j, w_down, (18 + 2 * j) * P, c)

            for t in range(TB):
                for c in range(2):
                    if c == 0:
                        sp.wait_ge(scalar_tile,
                                   count("scalar_tile", "down_b_end", 0, TAIL_TILES[t] + 4))
                    else:
                        sp.wait_ge(vector_tile,
                                   count("vector_tile", "down_b_end", 0, TB + 3 * t + 3))
                    sp.dma_start(out[t * P:(t + 1) * P, c * HALF:(c + 1) * HALF],
                                 tok(big_y, t, c)).then_inc(stored, 16)
            sp.wait_ge(stored, 16 * 2 * TB)

        @block.gpsimd
        def _(pool):
            nc.gpsimd.memset(ident[:], 0.0).then_inc(consts, 1)
            nc.gpsimd.memset(mask[:], 0.0).then_inc(consts, 1)
            nc.gpsimd.memset(op(SEL, H * P, slice(0, H)).bitcast(F32), 0.0).then_inc(consts, 1)
            nc.gpsimd.memset(ones[:], 1.0).then_inc(consts, 1)
            pool.wait_ge(consts, 4)
            nc.gpsimd.affine_select(out=ident[:], in_=ident[:], compare_op=ALU.not_equal, fill=1.0,
                                    base=0, pattern=[[-1, P]], channel_multiplier=1
                                    ).then_inc(consts, 1)
            nc.gpsimd.affine_select(out=mask[:], in_=mask[:], compare_op=ALU.is_ge, fill=NEG_INF,
                                    base=0, pattern=[[-1, P]], channel_multiplier=1
                                    ).then_inc(consts, 1)
            sel = op(SEL, H * P, slice(0, H)).rearrange("p (h c) -> p h c", h=H)
            nc.gpsimd.affine_select(out=sel, in_=sel.bitcast(F32), compare_op=ALU.not_equal,
                                    fill=-1.0, base=0, pattern=[[-1, H], [0, P]],
                                    channel_multiplier=1).then_inc(consts, 1)
            nc.gpsimd.iota(steps16[:], pattern=[[1, PAD]], base=1, channel_multiplier=0
                           ).then_inc(consts, 1)

        @block.tensor
        def _(pe):
            def begin(b, stage, i, k):
                before = count(f"free{b}", stage, i, k - 1)
                if not (isinstance(before, int) and before == 0):
                    pe.wait_ge(free[b], before)

            def product(b, s, blocks, hi, lo, first, last, width=S, ready=None):
                for n, (wb, k) in enumerate(blocks):
                    if ready is not None:
                        ready(k)
                    w = slice(wb * P, (wb + 1) * P)
                    a, z = first and n == 0, last and n == len(blocks) - 1
                    nc.tensor.matmul(banks[b][:, 0:width], whi[:, s, w], op(hi + k * S),
                                     start=a, stop=False)
                    nc.tensor.matmul(banks[b][:, 0:width], whi[:, s, w], op(lo + k * S),
                                     start=False, stop=False)
                    mm = nc.tensor.matmul(banks[b][:, 0:width], wlo[:, s, w], op(hi + k * S),
                                          start=False, stop=z)
                return mm

            def unit_ready(stage, i, j):
                n, s = unit(stage, i, j)
                pe.wait_ge(w_lo, n + 1)
                return s

            def whole(b, stage, i, j, k, hi, lo, ready=None):
                s = unit_ready(stage, i, j)
                begin(b, stage, i, k)
                mm = product(b, s, [(c, c) for c in range(UB)], hi, lo, True, True, ready=ready)
                mm.then_inc(used, 1)

            pe.wait_ge(const_in, 16 * 6)
            pe.wait_ge(consts, 8)
            nc.tensor.transpose(banks[7][:, 0:N_VECS], vec_rows, ident[0:N_VECS, 0:N_VECS]
                                ).then_inc(full[7], 1)
            for t in range(TB):
                pe.wait_ge(vector_tile, count("vector_tile", "norm", 0, H_ROWS[t]))
                for k in range(DB):
                    if t == 0 and k == 7:
                        begin(7, "norm", 0, 2)
                    tr = nc.tensor.transpose(banks[k][:, t * P:(t + 1) * P],
                                             big_y[:, t * D + k * P:t * D + (k + 1) * P], ident[:])
                    if t == TB - 1:
                        tr.then_inc(full[k], 1)

            def h_ready(k):
                wait_free(pe, k, "norm", 0, 1 if k < 7 else 2)

            def pool_map(g):
                pe.wait_ge(op_lo, count("op_lo", "front", 0, g + 1))
                if g == 0:
                    pe.wait_ge(pool_w_lo, 1)
                b, use, _ = POOL_MAP[g]
                begin(b, "front", 0, use)
                w = slice(g * P, (g + 1) * P)
                dh, dl = DF[g % 2]
                nc.tensor.matmul(banks[b][:], op(PW_HI)[:, w], op(dh), start=True, stop=False)
                nc.tensor.matmul(banks[b][:], op(PW_HI)[:, w], op(dl), start=False, stop=False)
                nc.tensor.matmul(banks[b][:], op(PW_LO)[:, w], op(dh), start=False, stop=True
                                 ).then_inc(full[b], 1)

            whole(0, "front", 0, 0, 1, H_HI, H_LO, h_ready)
            whole(1, "front", 0, 1, 1, H_HI, H_LO)
            whole(2, "front", 0, 2, 1, H_HI, H_LO)
            pool_map(0)
            whole(0, "front", 0, 3, 2, H_HI, H_LO)
            pool_map(1)
            whole(1, "front", 0, 4, 2, H_HI, H_LO)
            pe.wait_ge(vector_tile, count("vector_tile", "front", 0, 2))

            def spread_f(heads):
                for h in heads:
                    b = 4 + h % 4
                    begin(b, "front", 0, h // 4 + 1)
                    sel = op(SEL + h * P, P, slice(0, H))
                    nc.tensor.matmul(banks[b][:], sel, op(F_HI, S, slice(0, H)),
                                     start=True, stop=False)
                    nc.tensor.matmul(banks[b][:], sel, op(F_LO, S, slice(0, H)),
                                     start=False, stop=True).then_inc(full[b], 1)

            spread_f(range(4))
            begin(3, "front", 0, 2)
            for t in range(TB):
                tr = nc.tensor.transpose(banks[3][:, t * H:(t + 1) * H], fF[:, t * P:(t + 1) * P],
                                         ident[0:H, 0:H])
            tr.then_inc(full[3], 1)
            spread_f(range(4, H))
            pool_map(2)
            pool_map(3)

            with pe.Fori(0, WB) as i:
                whole(0, "pair", i, 0, 1, H_HI, H_LO)
                whole(1, "pair", i, 1, 1, H_HI, H_LO)
                s = unit_ready("pair", i, 2)
                begin(2, "pair", i, 1)
                product(2, s, [(c, c) for c in range(5)], H_HI, H_LO, True, False)
                wait_free(pe, 0, "pair", i, 1)
                wait_free(pe, 1, "pair", i, 1)
                pe.wait_ge(op_hi, count("op_hi", "pair", i, 3))
                for a in range(2):
                    if a == 1:
                        product(2, s, [(c, c) for c in (5, 6)], H_HI, H_LO, False, False)
                    rows = half_rows(a)
                    for b in range(TB):
                        begin(3 + b, "pair", i, a + 1)
                        n = max(b + 1, 2) * P
                        dst = banks[3 + b][:, 0:n]
                        nc.tensor.matmul(dst, op(QS[a] + b * P, P), op(KK[a], n),
                                         start=True, stop=False)
                        nc.tensor.matmul(dst, op(QS[a] + b * P, P, rows), op(K_LO, n, rows),
                                         start=False, stop=True).then_inc(full[3 + b], 1)
                product(2, s, [(7, 7)], H_HI, H_LO, False, True
                        ).then_inc(used, 1)
                whole(0, "pair", i, 3, 2, H_HI, H_LO)
                wait_free(pe, 2, "pair", i, 1)
                begin(7, "pair", i, 1)
                for t in range(TB):
                    tr = nc.tensor.transpose(banks[7][:, t * P:(t + 1) * P],
                                             wk(VT)[:, t * P:(t + 1) * P], ident[:])
                tr.then_inc(full[7], 1)
                whole(1, "pair", i, 4, 2, H_HI, H_LO)

                def turn_probs(a):
                    pe.wait_ge(probs, count("probs", "pair", i, a + 1))
                    for j in range(TB):
                        begin(3 + j, "pair", i, 3 + a)
                        for b in range(j, TB):
                            at = a * L_COLS + L_AT[b] + j * P
                            tr = nc.tensor.transpose(banks[3 + j][:, b * P:(b + 1) * P],
                                                     big_y[:, at:at + P], ident[:])
                        tr.then_inc(full[3 + j], 1)

                turn_probs(0)
                s = unit_ready("pair", i, 5)
                begin(2, "pair", i, 2)
                product(2, s, [(c, c) for c in range(6)], H_HI, H_LO, True, False)
                turn_probs(1)
                product(2, s, [(c, c) for c in range(6, 8)], H_HI, H_LO, False, True
                        ).then_inc(used, 1)

                for a, b, k in ((0, 7, 2), (1, 3, 5)):
                    wait_free(pe, 7, "pair", i, 1)
                    for j in range(TB):
                        wait_free(pe, 3 + j, "pair", i, 3 + a)
                    begin(b, "pair", i, k)
                    for j in range(TB):
                        first = min(j, TB - 2)
                        dst = banks[b][:, first * P:S]
                        n, at = S - first * P, PT_AT[j]
                        vj = slice(j * P, (j + 1) * P)
                        nc.tensor.matmul(dst, op(V_HI)[:, vj], op(PT[a][0] + at, n),
                                         start=(j == 0), stop=False)
                        nc.tensor.matmul(dst, op(V_HI)[:, vj], op(PT[a][1] + at, n),
                                         start=False, stop=False)
                        mm = nc.tensor.matmul(dst, op(V_LO)[:, vj], op(PT[a][0] + at, n),
                                              start=False, stop=(j == TB - 1))
                    mm.then_inc(full[b], 1)

            with pe.Fori(0, DB // 2) as i:
                def project(j, parts):
                    s = unit_ready("mix", i, j)
                    for half, (br, b, k) in enumerate(parts):
                        begin(b, "mix", i, k)
                        mm = product(b, s, [(half * WB + c, c) for c in range(WB)], *BR[br],
                                     True, True)
                    mm.then_inc(used, 1)

                whole(0, "mix", i, 0, 1, H_HI, H_LO)
                whole(1, "mix", i, 1, 1, H_HI, H_LO)
                wait_free(pe, 7, "pair", 3, 2)
                wait_free(pe, 3, "pair", 3, 5)
                project(2, [(0, 3, 1), (1, 4, 1)])
                whole(2, "mix", i, 3, 1, H_HI, H_LO)
                pe.wait_ge(op_lo, count("op_lo", "pair", 3, 1))
                project(4, [(2, 5, 1), (2, 6, 1)])
                whole(0, "mix", i, 5, 2, H_HI, H_LO)
                whole(1, "mix", i, 6, 2, H_HI, H_LO)
                project(7, [(0, 3, 2), (1, 4, 2)])
                whole(2, "mix", i, 8, 2, H_HI, H_LO)

            def rows_product(b, s, t, blocks, hi, lo, first, last):
                for q, k in enumerate(blocks):
                    w = slice(q * HALF, (q + 1) * HALF)
                    a, z = first and q == 0, last and q == 1
                    at = k * S + t * P
                    nc.tensor.matmul(banks[b][:], op(hi + at, P), whi[:, s, w],
                                     start=a, stop=False)
                    nc.tensor.matmul(banks[b][:], op(hi + at, P), wlo[:, s, w],
                                     start=False, stop=False)
                    mm = nc.tensor.matmul(banks[b][:], op(lo + at, P), whi[:, s, w],
                                          start=False, stop=z)
                return mm

            def turn_x1(c):
                for t in range(TB):
                    wait_free(pe, 4 * c + t, "out", 0, 1)
                for m in range(4 * c, 4 * c + 4):
                    for t in range(TB):
                        tr = nc.tensor.transpose(banks[m][:, t * P:(t + 1) * P],
                                                 big_x[:, t * D + m * P:t * D + (m + 1) * P],
                                                 ident[:])
                    tr.then_inc(full[m], 1)

            for j in range(8):
                c, n = j // 4, j % 4
                s = unit_ready("out", 0, j)
                if j == 0:
                    pe.wait_ge(op_lo, count("op_lo", "mix", 3, 1))
                if j == 3:
                    pe.wait_ge(op_lo, count("op_lo", "mix", 3, 2))
                for t in range(TB):
                    if n == 0:
                        begin(4 * c + t, "out", 0, 1)
                    mm = rows_product(4 * c + t, s, t, (2 * n, 2 * n + 1), MX_HI, MX_LO,
                                      n == 0, n == 3)
                    if n == 3 and t < TB - 1:
                        mm.then_inc(full[4 * c + t], 1)
                mm.then_inc(used, 1)
                if j == 4:
                    turn_x1(0)

            def x1_part(j, c):
                s = unit("ffn_first", 0, j)[1]
                if c == 0:
                    unit_ready("ffn_first", 0, j)
                    begin(j, "ffn_first", 0, 1)

                def split(k):
                    wait_free(pe, k, "out", 0, 2)

                mm = product(j, s, [(k, k) for k in range(4 * c, 4 * c + 4)], H_HI, H_LO,
                             c == 0, c == 1, ready=split)
                if c == 1:
                    mm.then_inc(used, 1)

            x1_part(0, 0)
            turn_x1(1)
            x1_part(1, 0)
            x1_part(0, 1)
            x1_part(1, 1)
            pe.wait_ge(vector_tile, count("vector_tile", "ffn_first", 0, 2))
            begin(6, "ffn_first", 0, 1)
            nc.tensor.matmul(banks[6][:], ones[:, 0:P], DIAG, start=True, stop=True
                             ).then_inc(full[6], 1)
            with pe.Fori(0, 7) as i:
                for j in range(3):
                    a = (2 * j + 2) % 6
                    whole(a, "ffn", i, 2 * j, 1, H_HI, H_LO)
                    whole(a + 1, "ffn", i, 2 * j + 1, 1, H_HI, H_LO)

            pe.wait_ge(op_lo, count("op_lo", "ffn", 6, 2))
            for c, part in enumerate("ab"):
                units = [(f"down_{part}", n // 3, n % 3) for n in range(9)]
                units += [(f"down_{part}_end", 0, j) for j in range(2)]
                end = f"down_{part}_end"
                apart = 11 if c == 0 else 8
                for n, (stage, i, j) in enumerate(units[:apart]):
                    s = unit_ready(stage, i, j)
                    if n == 10:
                        pe.wait_ge(op_lo, count("op_lo", "ffn", 6, 3))
                    for t in range(TB):
                        b = DOWN_BANKS[c][t]
                        if n == 0:
                            begin(b, end, 0, 1)
                        mm = rows_product(b, s, t, (2 * n, 2 * n + 1), HID_HI, HID_LO,
                                          n == 0, n == 10)
                        if n == 10 and t < TB - 1:
                            mm.then_inc(full[b], 1)
                    mm.then_inc(used, 1)
                if c == 1:
                    slots = {8: unit_ready(*units[8]), 9: unit_ready(*units[9])}
                    for t, n in [(0, 8), (0, 9), (1, 8), (1, 9), (0, 10), (1, 10), (2, 8), (2, 9),
                                 (2, 10), (3, 8), (3, 9), (3, 10)]:
                        if n not in slots:
                            slots[n] = unit_ready(*units[n])
                        b = DOWN_BANKS[c][t]
                        mm = rows_product(b, slots[n], t, (2 * n, 2 * n + 1), HID_HI, HID_LO,
                                          False, n == 10)
                        if n == 10:
                            mm.then_inc(full[b], 1)

        @block.scalar
        def _(act):
            def split_hi(stage, i, j):
                n, s = unit(stage, i, j)
                act.wait_ge(landed[s], 32 * loads_before(stage, i, j))
                if not (stage == "front" and n < SLOTS):
                    act.wait_ge(used, n - SLOTS + 1)
                nc.scalar.copy(whi[:, s, :], raw[:, s, :]).then_inc(w_hi, 1)

            def operand_hi(dst, src, scale=1.0):
                nc.scalar.activation(dst, src, ACT.Copy, scale=scale).then_inc(op_hi, 1)

            def tile(dst, src, func, **kw):
                return nc.scalar.activation(dst, src, func, **kw).then_inc(scalar_tile, 1)

            nc.scalar.preload_act_table_set("natural_log_exp_and_others")
            def square(t):
                act.wait_ge(x_in[t], 16)
                tile(big_y[:, t * D:(t + 1) * D], big_x[:, t * D:(t + 1) * D], ACT.Square,
                     accum_out=stat[:, t:t + 1])

            square(0)
            for t in range(TB):
                if t + 1 < TB:
                    square(t + 1)
                act.wait_ge(vector_tile, count("vector_tile", "norm", 0, VARIANCE[t]))
                tile(stat[:, 8 + t:9 + t], stat[:, 4 + t:5 + t], ACT.Ln)
                act.wait_ge(scalar_tile, count("scalar_tile", "norm", 0, RSQRT[t] - 1))
                tile(stat[:, 12 + t:13 + t], stat[:, 8 + t:9 + t], ACT.Exp, scale=-0.5)
            split_hi("front", 0, 0)
            split_hi("front", 0, 1)
            wait_free(act, 7, "norm", 0, 1)
            for k in range(DB):
                wait_full(act, k, "norm", 0, 1 if k < 7 else 2)
                operand_hi(op(H_HI + k * S), banks[k][:], vecs[:, V_ATTN + k:V_ATTN + k + 1])
            split_hi("front", 0, 2)

            split_hi("front", 0, 3)
            act.wait_ge(vector_tile, count("vector_tile", "front", 0, 1))
            tile(fe, fe, ACT.Exp, scale=-1.0)
            act.wait_ge(scalar_tile, count("scalar_tile", "front", 0, 1))
            tile(fe, fe, ACT.Ln, bias=1.0)
            act.wait_ge(pool_w_in, 16)
            nc.scalar.copy(op(PW_HI), pw_raw).then_inc(pool_w_hi, 1)

            def pool_out(g):
                b, _, filled = POOL_MAP[g]
                wait_full(act, b, "front", 0, filled)
                operand_hi(op(BR[1][0] + g * S), banks[b][:], vecs[:, V_SCALE + g:V_SCALE + g + 1])

            def diff_hi(g):
                if g >= 2:
                    b, _, filled = POOL_MAP[g - 2]
                    wait_full(act, b, "front", 0, filled)
                wait_free(act, (1, 2, 0, 1)[g], "front", 0, (1, 1, 2, 2)[g])
                operand_hi(op(DF[g % 2][0]), diff)

            def copy_f(heads):
                for h in heads:
                    b = 4 + h % 4
                    wait_full(act, b, "front", 0, h // 4 + 1)
                    nc.scalar.copy(big_x[:, h * S:(h + 1) * S], banks[b][:]).then_inc(free[b], 1)

            diff_hi(0)
            split_hi("front", 0, 4)
            pool_out(0)
            diff_hi(1)
            split_hi("front", 0, 5)
            pool_out(1)
            diff_hi(2)
            split_hi("front", 0, 6)
            copy_f(range(4))
            diff_hi(3)
            pool_out(2)
            copy_f(range(4, H))
            split_hi("front", 0, 7)
            pool_out(3)

            with act.Fori(0, WB) as i:
                wait_unit(act, "pair", i, 0)
                for a in range(2):
                    rows = half_rows(a)
                    ins = nc.scalar.activation(op(QS[a], S, rows), banks[0][rows, :], ACT.Copy,
                                               scale=SCALE)
                ins.then_inc(op_hi, 1)
                split_hi("pair", i, 3)
                wait_unit(act, "pair", i, 1)
                for a in range(2):
                    ins = nc.scalar.activation(op(KK[a], S, half_rows(a)),
                                               banks[1][half_rows(a), :], ACT.Copy)
                ins.then_inc(op_hi, 1)
                act.wait_ge(op_hi, count("op_hi", "pair", i, 2))
                for a in range(2):
                    ins = nc.scalar.copy(op(KK[a], S, half_rows(1 - a)),
                                         op(KK[a], S, half_rows(a)).bitcast(F32))
                ins.then_inc(op_hi, 1)
                split_hi("pair", i, 4)
                for a in range(2):
                    act.wait_ge(row_max, count("row_max", "pair", i, a + 1))
                    for b in range(TB):
                        lg = big_y[:, a * L_COLS + L_AT[b]:a * L_COLS + L_AT[b] + (b + 1) * P]
                        at = 4 * a + b
                        e = nc.scalar.activation(lg, lg, ACT.Exp, bias=stat[:, 16 + at:17 + at],
                                                 accum_out=stat[:, 24 + at:25 + at])
                    e.then_inc(exp_done, 1)
                    if a == 0:
                        wait_unit(act, "pair", i, 2)
                        nc.scalar.copy(wk(VT), banks[2][:]).then_inc(free[2], 1)
                        split_hi("pair", i, 5)
                wait_unit(act, "pair", i, 3)
                nc.scalar.copy(wk(CV), banks[0][:]).then_inc(free[0], 1)
                wait_full(act, 7, "pair", i, 1)
                operand_hi(op(V_HI), banks[7][:])
                split_hi("pair", i, 6)
                wait_unit(act, "pair", i, 4)
                nc.scalar.copy(wk(CB), banks[1][:]).then_inc(free[1], 1)
                split_hi("pair", i, 7)
                for a in range(2):
                    for j in range(TB):
                        wait_full(act, 3 + j, "pair", i, 3 + a)
                        operand_hi(op(PT[a][0] + pt_at(j), S - j * P), banks[3 + j][:, j * P:S])
                for a, b, k in ((0, 7, 2), (1, 3, 5)):
                    rows = slice(a * HD, (a + 1) * HD)
                    wait_full(act, b, "pair", i, k)
                    operand_hi(operands[rows, bass.ds(BR[0][0] + i * S, S)], banks[b][rows, :])
                act.wait_ge(vector_tile, count("vector_tile", "pair", i, 1))
                operand_hi(opd(BR[2][0], i), wk(CY))
                split_hi("pair", i, 8)

            nc.scalar.preload_act_table(ACT.Sigmoid)
            with act.Fori(0, DB // 2) as i:
                def gate(j, b, k, br, mm):
                    wait_unit(act, "mix", i, j)
                    if mm == 0:
                        wait_free(act, (3, 4, 6)[br], "mix", i, 0)
                    else:
                        wait_free(act, (3, 4, 5)[br], "mix", i, 1)
                    nc.scalar.activation(wk(GA + br), banks[b][:], ACT.Sigmoid,
                                         bias=vecs[:, bass.ds(i * 2 + (V_GATE + br * DB + mm), 1)]
                                         ).then_inc(free[b], 1)

                def merged_hi(mm):
                    act.wait_ge(vector_tile, count("vector_tile", "mix", i, mm + 1))
                    operand_hi(opd(MX_HI, i * 2 + mm), wk(ACC))

                gate(0, 0, 1, 0, 0)
                split_hi("mix", i, 3)
                gate(1, 1, 1, 1, 0)
                split_hi("mix", i, 4)
                split_hi("mix", i, 5)
                gate(3, 2, 1, 2, 0)
                split_hi("mix", i, 6)
                merged_hi(0)
                split_hi("mix", i, 7)
                gate(5, 0, 2, 0, 1)
                split_hi("mix", i, 8)
                gate(6, 1, 2, 1, 1)
                split_hi("mix", i, 9)
                split_hi("mix", i, 10)
                gate(8, 2, 2, 2, 1)
                merged_hi(1)
                split_hi("mix", i, 11)

            def squares(stage, banks_of, junk, at, t, before):
                c = 0 if at in (SS_OUT, SS_DOWN) else 1
                wait_free(act, banks_of[t], stage, 0, 1)
                act.wait_ge(scalar_tile, count("scalar_tile", stage, 0, before))
                tile(wk(junk), tok(big_x, t, c), ACT.Square,
                     accum_out=stat[:, at + t:at + t + 1])

            def x1_hi(m):
                wait_full(act, m, "out", 0, 1 if m in (3, 7) else 2)
                operand_hi(op(H_HI + m * S), banks[m][:], vecs[:, V_FFN + m:V_FFN + m + 1])

            for j in (3, 4, 5):
                split_hi("out", 0, j)
            for t in range(TB):
                squares("out", range(0, 4), JUNK_OUT, SS_OUT, t, t)
            split_hi("out", 0, 6)
            split_hi("out", 0, 7)
            for m in range(4):
                x1_hi(m)
            split_hi("out", 0, 8)
            split_hi("out", 0, 9)
            for t in range(TB):
                squares("out", range(4, 8), JUNK_OUT, SS_OUT + 4, t, 4 + t)
            split_hi("out", 0, 10)
            for m in range(4, 8):
                x1_hi(m)

            def hidden(stage, i, j, a):
                wait_free(act, a, stage, i, 1)
                done = j + 1 if stage == "ffn" else 3
                tile(wk(SG), wk(A1), ACT.Sigmoid)
                split_hi(stage, i, 2 * j + 3)
                act.wait_ge(vector_tile, count("vector_tile", stage, i, done))
                hb = i * 3 + (1 + j) if stage == "ffn" else 0
                operand_hi(opd(HID_HI, hb), wk(HD_))
                split_hi(stage, i, 2 * j + 4)

            nc.scalar.preload_act_table_set("natural_log_exp_and_others")
            act.wait_ge(vector_tile, count("vector_tile", "ffn_first", 0, 1))
            tile(stat[:, 8:12], stat[:, 4:8], ACT.Ln)
            act.wait_ge(scalar_tile, count("scalar_tile", "ffn_first", 0, 1))
            tile(stat[:, 12:16], stat[:, 8:12], ACT.Exp, scale=-0.5)
            nc.scalar.preload_act_table(ACT.Sigmoid)
            wait_full(act, 6, "ffn_first", 0, 1)
            nc.scalar.copy(RSTD, banks[6][:]).then_inc(free[6], 1)
            hidden("ffn_first", 0, 0, 0)
            with act.Fori(0, 7) as i:
                for j in range(3):
                    hidden("ffn", i, j, (2 * j + 2) % 6)

            nc.scalar.preload_act_table_set("natural_log_exp_and_others")
            with act.Fori(0, 3) as i:
                for j in range(3, 6):
                    split_hi("down_a", i, j)
            split_hi("down_a_end", 0, 3)
            split_hi("down_a_end", 0, 4)
            for t in range(TB):
                squares("down_a_end", DOWN_BANKS[0], JUNK, SS_DOWN, t, t)
            with act.Fori(0, 2) as i:
                for j in range(3, 6):
                    split_hi("down_b", i, j)
            split_hi("down_b", 2, 3)
            split_hi("down_b", 2, 4)
            for t in range(TB):
                squares("down_b_end", DOWN_BANKS[1], JUNK, SS_DOWN + 4, t, TAIL_TILES[t])
                act.wait_ge(vector_tile, count("vector_tile", "down_b_end", 0, TB + 3 * t + 1))
                tile(stat[:, 8 + t:9 + t], stat[:, 4 + t:5 + t], ACT.Ln)
                act.wait_ge(scalar_tile, count("scalar_tile", "down_b_end", 0, TAIL_TILES[t] + 2))
                tile(stat[:, 12 + t:13 + t], stat[:, 8 + t:9 + t], ACT.Exp, scale=-0.5)
                act.wait_ge(vector_tile, count("vector_tile", "down_b_end", 0, TB + 3 * t + 2))
                tile(tok(big_y, t, 0), tok(big_x, t, 0), ACT.Copy, scale=stat[:, t:t + 1])

        @block.vector
        def _(dve):
            where = {}

            def enter(stage, i=0):
                if where:
                    leave()
                where.update(stage=stage, i=i, steps=0)

            def leave():
                want = RAISED["vector_step"].get(where["stage"], 0)
                assert where["steps"] == want, (where, want)

            def step(ins):
                where["steps"] += 1
                ins.then_inc(vector_step, 1)
                dve.wait_ge(vector_step, count("vector_step", where["stage"], where["i"],
                                               where["steps"]))

            def split_lo(stage, i, j):
                n, s = unit(stage, i, j)
                dve.wait_ge(w_hi, n + 1)
                nc.vector.tensor_tensor(wlo[:, s, :], raw[:, s, :], whi[:, s, :].bitcast(F32),
                                        ALU.subtract).then_inc(w_lo, 1)

            def operand_lo(stage, i, k, hi, lo, src, scale=None, bank=None):
                dve.wait_ge(op_hi, count("op_hi", stage, i, k))
                if scale is None:
                    ins = nc.vector.tensor_tensor(lo, src, hi.bitcast(F32), ALU.subtract)
                else:
                    ins = nc.vector.scalar_tensor_tensor(out=lo, in0=src, scalar=scale,
                                                         in1=hi.bitcast(F32), op0=ALU.mult,
                                                         op1=ALU.subtract)
                ins.then_inc(op_lo if bank is None else free[bank], 1)

            def newton(rstd, var, tmp, out):
                step(nc.vector.tensor_tensor(tmp, var, rstd, ALU.mult))
                step(nc.vector.tensor_tensor(tmp, tmp, rstd, ALU.mult))
                step(nc.vector.tensor_scalar(tmp, tmp, -0.5, 1.5, ALU.mult, ALU.add))
                return nc.vector.tensor_tensor(out, tmp, rstd, ALU.mult)

            def newton_column(rstd, var, tmp, out):
                step(nc.vector.scalar_tensor_tensor(out=tmp, in0=var, scalar=rstd, in1=rstd,
                                                    op0=ALU.mult, op1=ALU.mult))
                step(nc.vector.tensor_scalar(tmp, tmp, -0.5, 1.5, ALU.mult, ALU.add))
                return nc.vector.tensor_tensor(out, tmp, rstd, ALU.mult)

            enter("norm")
            dve.wait_ge(consts, 8)
            step(nc.vector.tensor_copy(recip16[:], steps16[:]))
            step(nc.vector.reciprocal(recip16[:], recip16[:]))
            for g, w in enumerate(POOL_WINDOWS):
                step(nc.vector.tensor_scalar(inv16[:, g, :], recip16[:], 1.0 / w, None, ALU.max))
            step(nc.vector.memset(cum[:, 0:PAD], 0.0))
            def mean_square(t):
                dve.wait_ge(scalar_tile, count("scalar_tile", "norm", 0, SQUARED[t]))
                nc.vector.tensor_scalar(stat[:, 4 + t:5 + t], stat[:, t:t + 1], 1.0 / D, EPS,
                                        ALU.mult, ALU.add).then_inc(vector_tile, 1)

            mean_square(0)
            for t in range(TB):
                if t + 1 < TB:
                    mean_square(t + 1)
                if t == 1:
                    wait_full(dve, 7, "norm", 0, 1)
                    nc.vector.tensor_copy(vecs[:], banks[7][:, 0:N_VECS]).then_inc(free[7], 1)
                    wait_free(dve, 7, "norm", 0, 1)
                ss, var, tmp, rstd = [stat[:, c + t:c + t + 1] for c in (0, 4, 8, 12)]
                dve.wait_ge(vector_tile, count("vector_tile", "norm", 0, VARIANCE[t]))
                dve.wait_ge(scalar_tile, count("scalar_tile", "norm", 0, RSQRT[t]))
                step(newton_column(rstd, var, tmp, ss))
                nc.vector.tensor_scalar(big_y[:, t * D:(t + 1) * D], big_x[:, t * D:(t + 1) * D],
                                        ss, None, ALU.mult).then_inc(vector_tile, 1)
            split_lo("front", 0, 0)
            for k in range(DB):
                operand_lo("norm", 0, k + 1, op(H_HI + k * S), op(H_LO + k * S), banks[k][:],
                           vecs[:, V_ATTN + k:V_ATTN + k + 1], k)
            split_lo("front", 0, 1)
            split_lo("front", 0, 2)

            enter("front")
            wait_unit(dve, "front", 0, 0)
            nc.vector.tensor_scalar(fz, banks[0][0:H, :], bias_f[:, 0:1], None, ALU.add
                                    ).then_inc(free[0], 1)
            wait_free(dve, 0, "front", 0, 1)
            nc.vector.scalar_tensor_tensor(out=fe, in0=fz, scalar=-1.0, in1=fz, op0=ALU.mult,
                                           op1=ALU.max).then_inc(vector_tile, 1)

            def pool_diff(g, j, bank, k):
                w = POOL_WINDOWS[g]
                wait_unit(dve, "front", 0, j)
                step(nc.vector.tensor_tensor_scan(cum[:, PAD:], ones[:], banks[bank][:], 0.0,
                                                  ALU.mult, ALU.add))
                step(nc.vector.tensor_tensor(diff, cum[:, PAD:], cum[:, PAD - w:PAD + S - w],
                                             ALU.subtract))
                step(nc.vector.tensor_tensor(edge[:], diff[:, 0:PAD], inv16[:, g, :], ALU.mult))
                step(nc.vector.scalar_tensor_tensor(out=diff, in0=diff, scalar=1.0 / w,
                                                    in1=banks[bank][:], op0=ALU.mult,
                                                    op1=ALU.subtract))
                nc.vector.tensor_tensor(diff[:, 0:PAD], edge[:], banks[bank][:, 0:PAD],
                                        ALU.subtract).then_inc(free[bank], 1)

            def diff_lo(g, k):
                operand_lo("front", 0, k, op(DF[g % 2][0]), op(DF[g % 2][1]), diff)

            def pool_lo(g, k):
                b = POOL_MAP[g][0]
                operand_lo("front", 0, k, op(BR[1][0] + g * S), op(BR[1][1] + g * S), banks[b][:],
                           vecs[:, V_SCALE + g:V_SCALE + g + 1], b)

            split_lo("front", 0, 3)
            dve.wait_ge(scalar_tile, count("scalar_tile", "front", 0, 2))
            step(nc.vector.scalar_tensor_tensor(out=fz, in0=fz, scalar=0.0, in1=fe, op0=ALU.min,
                                                op1=ALU.subtract))
            step(nc.vector.tensor_tensor_scan(fF, ones[0:H, :], fz, 0.0, ALU.mult, ALU.add))
            step(nc.vector.tensor_copy(op(F_HI, S, slice(0, H)), fF))
            nc.vector.tensor_tensor(op(F_LO, S, slice(0, H)), fF,
                                    op(F_HI, S, slice(0, H)).bitcast(F32), ALU.subtract
                                    ).then_inc(vector_tile, 1)
            pool_diff(0, 1, 1, 1)
            diff_lo(0, 1)
            dve.wait_ge(pool_w_hi, 1)
            nc.vector.tensor_tensor(op(PW_LO), pw_raw, op(PW_HI).bitcast(F32), ALU.subtract
                                    ).then_inc(pool_w_lo, 1)
            dve.wait_ge(op_lo, 1)
            pool_diff(1, 2, 2, 1)
            split_lo("front", 0, 4)
            pool_lo(0, 2)
            diff_lo(1, 3)
            dve.wait_ge(op_lo, 2)
            pool_diff(2, 3, 0, 2)
            split_lo("front", 0, 5)
            pool_lo(1, 4)
            diff_lo(2, 5)
            dve.wait_ge(op_lo, 3)
            pool_diff(3, 4, 1, 2)
            wait_full(dve, 3, "front", 0, 2)
            nc.vector.tensor_copy(f_rows[:].rearrange("p t h -> p (t h)"), banks[3][:, 0:TB * H]
                                  ).then_inc(free[3], 1)
            diff_lo(3, 6)
            split_lo("front", 0, 6)
            pool_lo(2, 7)
            split_lo("front", 0, 7)
            pool_lo(3, 8)
            for b in range(4, 8):
                wait_full(dve, b, "front", 0, 2)
            for a in range(2):
                for half in PT[a]:
                    zeros = op(half + PT_AT[TB - 1], P).bitcast(F32)
                    step(nc.vector.memset(zeros, 0.0))

            with dve.Fori(0, WB) as i:
                enter("pair", i)
                dve.wait_ge(op_hi, count("op_hi", "pair", i, 1))
                for a in range(2):
                    rows = half_rows(a)
                    ins = nc.vector.scalar_tensor_tensor(
                        out=op(QS[a], S, half_rows(1 - a)), in0=banks[0][rows, :], scalar=SCALE,
                        in1=op(QS[a], S, rows).bitcast(F32), op0=ALU.mult, op1=ALU.subtract)
                ins.then_inc(free[0], 1)
                split_lo("pair", i, 3)
                dve.wait_ge(op_hi, count("op_hi", "pair", i, 2))
                for a in range(2):
                    rows = half_rows(a)
                    ins = nc.vector.tensor_tensor(op(K_LO, S, rows), banks[1][rows, :],
                                                  op(KK[a], S, rows).bitcast(F32), ALU.subtract)
                ins.then_inc(free[1], 1)
                split_lo("pair", i, 4)
                for b in range(3, 8):
                    wait_free(dve, b, "front", 0, RAISED[f"free{b}"]["front"])
                for a in range(2):
                    lg = big_y[:, a * L_COLS:(a + 1) * L_COLS]
                    for b in range(TB):
                        n = (b + 1) * P
                        wait_full(dve, 3 + b, "pair", i, a + 1)
                        nc.vector.scalar_tensor_tensor(
                            out=lg[:, L_AT[b]:L_AT[b] + n],
                            in0=big_x[:, bass.ds(i * (2 * S) + a * S, n)],
                            scalar=f_rows[:, b, bass.ds(i * 2 + a, 1)],
                            in1=banks[3 + b][:, 0:n], op0=ALU.add, op1=ALU.add
                            ).then_inc(free[3 + b], 1)
                    for b in range(TB):
                        wait_free(dve, 3 + b, "pair", i, a + 1)
                    diag = lg.rearrange("p (a c) -> p a c", c=P)[:, 0:13:4, :]
                    step(nc.vector.tensor_tensor(
                        diag, diag, mask[:].rearrange("p (a c) -> p a c", a=1)
                        .to_broadcast([P, TB, P]), ALU.add))
                    for b in range(TB):
                        step(nc.vector.tensor_reduce(
                            stat[:, 32 + 4 * a + b:33 + 4 * a + b],
                            lg[:, L_AT[b]:L_AT[b] + (b + 1) * P], AX_X, ALU.max))
                    nc.vector.tensor_scalar(stat[:, 16 + 4 * a:20 + 4 * a],
                                            stat[:, 32 + 4 * a:36 + 4 * a], -1.0, None, ALU.mult
                                            ).then_inc(row_max, 1)
                for a in range(2):
                    dve.wait_ge(exp_done, count("exp_done", "pair", i, a + 1))
                    step(nc.vector.reciprocal(stat[:, 40 + 4 * a:44 + 4 * a],
                                              stat[:, 24 + 4 * a:28 + 4 * a]))
                    for b in range(TB):
                        at = a * L_COLS + L_AT[b]
                        lg = big_y[:, at:at + (b + 1) * P]
                        ins = nc.vector.tensor_scalar(lg, lg, stat[:, 40 + 4 * a + b:41 + 4 * a + b],
                                                      None, ALU.mult)
                    ins.then_inc(probs, 1)
                split_lo("pair", i, 5)
                operand_lo("pair", i, 4, op(V_HI), op(V_LO), banks[7][:], None, 7)
                split_lo("pair", i, 6)
                split_lo("pair", i, 7)
                for a in range(2):
                    for j in range(TB):
                        operand_lo("pair", i, 5 + 4 * a + j,
                                   op(PT[a][0] + pt_at(j), S - j * P),
                                   op(PT[a][1] + pt_at(j), S - j * P),
                                   banks[3 + j][:, j * P:S], None, 3 + j)
                wait_unit(dve, "pair", i, 5)
                wait_free(dve, 0, "pair", i, 2)
                nc.vector.tensor_tensor(wk(CV), banks[2][:], wk(CV), ALU.mult
                                        ).then_inc(free[2], 1)
                wait_free(dve, 2, "pair", i, 2)
                for a, b in ((0, 7), (1, 3)):
                    rows = slice(a * HD, (a + 1) * HD)
                    operand_lo("pair", i, 13 + a, operands[rows, bass.ds(BR[0][0] + i * S, S)],
                               operands[rows, bass.ds(BR[0][1] + i * S, S)], banks[b][rows, :],
                               None, b)

                def tap(k):
                    return vecs[:, bass.ds(i + (V_CONV + k * WB), 1)]

                dve.wait_ge(op_lo, count("op_lo", "pair", i, 0))
                step(nc.vector.tensor_scalar(wk(CY), wk(CV), tap(2), None, ALU.mult))
                for k in (1, 0):
                    lag = 2 - k
                    step(nc.vector.scalar_tensor_tensor(
                        out=wk(CY)[:, lag:S], in0=wk(CV)[:, 0:S - lag], scalar=tap(k),
                        in1=wk(CY)[:, lag:S], op0=ALU.mult, op1=ALU.add))
                wait_free(dve, 1, "pair", i, 2)
                nc.vector.tensor_tensor(wk(CY), wk(CY), wk(CB), ALU.mult
                                        ).then_inc(vector_tile, 1)
                operand_lo("pair", i, 15, opd(BR[2][0], i), opd(BR[2][1], i), wk(CY))
                split_lo("pair", i, 8)

            with dve.Fori(0, DB // 2) as i:
                enter("mix", i)

                def gated(dst, j, b, k, br, mm):
                    wait_unit(dve, "mix", i, j)
                    wait_free(dve, br, "mix", i, 1 + mm)
                    nc.vector.tensor_tensor(dst, banks[b][:], wk(GA + br), ALU.mult
                                            ).then_inc(free[b], 1)
                    return lambda: wait_free(dve, b, "mix", i, k)

                for mm in range(2):
                    split_lo("mix", i, 3 + 5 * mm)
                    split_lo("mix", i, 4 + 5 * mm)
                    dve.wait_ge(op_lo, count("op_lo", "mix", i, mm))
                    first = gated(wk(ACC), 2 + 5 * mm, 3, 1 + mm, 0, mm)
                    second = gated(wk(TMP), 2 + 5 * mm, 4, 1 + mm, 1, mm)
                    first()
                    second()
                    step(nc.vector.tensor_tensor(wk(ACC), wk(ACC), wk(TMP), ALU.add))
                    split_lo("mix", i, 5 + 5 * mm)
                    if mm == 0:
                        split_lo("mix", i, 6)
                    gated(wk(TMP), 4, 5 + mm, 1, 2, mm)()
                    nc.vector.tensor_tensor(wk(ACC), wk(ACC), wk(TMP), ALU.add
                                            ).then_inc(vector_tile, 1)
                    operand_lo("mix", i, 1 + mm, opd(MX_HI, i * 2 + mm), opd(MX_LO, i * 2 + mm),
                               wk(ACC))
                    split_lo("mix", i, 7 if mm == 0 else 11)

            def residual(stage, c, b, t, other):
                nc.vector.tensor_tensor(tok(big_x, t, c), banks[b][:], tok(other, t, c), ALU.add
                                        ).then_inc(free[b], 1)

            def x1_half(c):
                for t in range(TB):
                    b = 4 * c + t
                    if t < TB - 1:
                        wait_full(dve, b, "out", 0, 1)
                    else:
                        wait_unit(dve, "out", 0, 4 * c + 3)
                    dve.wait_ge(x_again[t], 16)
                    residual("out", c, b, t, big_y)

            def x1_lo(m):
                operand_lo("out", 0, m + 1, op(H_HI + m * S), op(H_LO + m * S), banks[m][:],
                           vecs[:, V_FFN + m:V_FFN + m + 1], m)

            enter("out")
            for j in (3, 4, 5):
                split_lo("out", 0, j)
            x1_half(0)
            split_lo("out", 0, 6)
            split_lo("out", 0, 7)
            for m in range(4):
                x1_lo(m)
            split_lo("out", 0, 8)
            split_lo("out", 0, 9)
            x1_half(1)
            split_lo("out", 0, 10)
            for m in range(4, 8):
                x1_lo(m)

            enter("ffn_first")
            dve.wait_ge(scalar_tile, count("scalar_tile", "out", 0, 8))
            step(nc.vector.tensor_tensor(stat[:, 0:4], stat[:, SS_OUT:SS_OUT + 4],
                                         stat[:, SS_OUT + 4:SS_OUT + 8], ALU.add))
            nc.vector.tensor_scalar(stat[:, 4:8], stat[:, 0:4], 1.0 / D, EPS, ALU.mult, ALU.add
                                    ).then_inc(vector_tile, 1)
            dve.wait_ge(vector_tile, count("vector_tile", "ffn_first", 0, 1))
            dve.wait_ge(scalar_tile, count("scalar_tile", "ffn_first", 0, 2))
            step(newton(stat[:, 12:16], stat[:, 4:8], stat[:, 8:12], stat[:, 0:4]))
            for t in range(TB):
                ins = nc.vector.tensor_scalar(DIAG[:, t * P:(t + 1) * P], ident[:],
                                              stat[:, t:t + 1], None, ALU.mult)
            ins.then_inc(vector_tile, 1)
            wait_free(dve, 6, "ffn_first", 0, 1)

            def hidden(stage, i, j, a):
                wait_unit(dve, stage, i, 2 * j)
                nc.vector.tensor_tensor(wk(A1), banks[a][:], RSTD, ALU.mult).then_inc(free[a], 1)
                split_lo(stage, i, 2 * j + 3)
                wait_unit(dve, stage, i, 2 * j + 1)
                nc.vector.tensor_tensor(wk(B1), banks[a + 1][:], RSTD, ALU.mult
                                        ).then_inc(free[a + 1], 1)
                wait_free(dve, a, stage, i, 1)
                dve.wait_ge(scalar_tile, count("scalar_tile", stage, i,
                                               j + 1 if stage == "ffn" else 3))
                dve.wait_ge(op_lo, count("op_lo", stage, i, j))
                step(nc.vector.tensor_tensor(wk(HD_), wk(A1), wk(SG), ALU.mult))
                wait_free(dve, a + 1, stage, i, 1)
                nc.vector.tensor_tensor(wk(HD_), wk(HD_), wk(B1), ALU.mult
                                        ).then_inc(vector_tile, 1)
                hb = i * 3 + (1 + j) if stage == "ffn" else 0
                operand_lo(stage, i, j + 1, opd(HID_HI, hb), opd(HID_LO, hb), wk(HD_))
                split_lo(stage, i, 2 * j + 4)

            hidden("ffn_first", 0, 0, 0)
            with dve.Fori(0, 7) as i:
                enter("ffn", i)
                for j in range(3):
                    hidden("ffn", i, j, (2 * j + 2) % 6)

            with dve.Fori(0, 3) as i:
                for j in range(3, 6):
                    split_lo("down_a", i, j)
            split_lo("down_a_end", 0, 3)
            for t in range(TB):
                if t < TB - 1:
                    wait_full(dve, DOWN_BANKS[0][t], "down_a_end", 0, 1)
                else:
                    wait_unit(dve, "down_a_end", 0, 1)
                residual("down_a_end", 0, DOWN_BANKS[0][t], t, big_x)
            split_lo("down_a_end", 0, 4)
            with dve.Fori(0, 2) as i:
                for j in range(3, 6):
                    split_lo("down_b", i, j)
            split_lo("down_b", 2, 3)
            split_lo("down_b", 2, 4)

            enter("down_b_end")
            dve.wait_ge(final_g_in, 16)
            dve.wait_ge(scalar_tile, count("scalar_tile", "down_a_end", 0, 4))
            step(nc.vector.tensor_scalar(stat[:, 16:20], stat[:, SS_DOWN:SS_DOWN + 4],
                                         1.0 / D, EPS, ALU.mult, ALU.add))
            for t in range(TB):
                nc.vector.tensor_tensor(tok(big_x, t, 0), tok(big_x, t, 0), final_g[:, 0:HALF],
                                        ALU.mult).then_inc(vector_tile, 1)

            def x2_last(t):
                wait_full(dve, DOWN_BANKS[1][t], "down_b_end", 0, 1)
                residual("down_b_end", 1, DOWN_BANKS[1][t], t, big_x)

            x2_last(0)
            for t in range(TB):
                ss, var, tmp, rstd, first = [stat[:, col + t:col + t + 1]
                                             for col in (0, 4, 8, 12, 16)]
                dve.wait_ge(scalar_tile, count("scalar_tile", "down_b_end", 0, TAIL_TILES[t] + 1))
                square_sum = stat[:, SS_DOWN + 4 + t:SS_DOWN + 5 + t]
                nc.vector.scalar_tensor_tensor(out=var, in0=square_sum, scalar=1.0 / D, in1=first,
                                               op0=ALU.mult, op1=ALU.add).then_inc(vector_tile, 1)
                dve.wait_ge(vector_tile, count("vector_tile", "down_b_end", 0, TB + 3 * t + 1))
                dve.wait_ge(scalar_tile, count("scalar_tile", "down_b_end", 0, TAIL_TILES[t] + 3))
                newton_column(rstd, var, tmp, ss).then_inc(vector_tile, 1)
                dve.wait_ge(vector_tile, count("vector_tile", "down_b_end", 0, TB + 3 * t + 2))
                if t == TB - 2:
                    x2_last(t + 1)
                nc.vector.scalar_tensor_tensor(
                    out=tok(big_y, t, 1), in0=tok(big_x, t, 1), scalar=ss,
                    in1=final_g[:, HALF:D], op0=ALU.mult, op1=ALU.mult
                    ).then_inc(vector_tile, 1)
                if t < TB - 2:
                    x2_last(t + 1)
            leave()


_INS = ["x", "attn_norm", "w_in", "b_forget", "b_gate", "w_proj_attn", "pool_w", "pool_scale",
        "w_proj_pool", "conv_w", "w_proj_conv", "w_out", "ffn_norm", "w_gate_up", "w_down",
        "final_norm"]


def kernel(**inputs):
    import numpy as _np
    import concourse.bacc as _bacc
    from concourse import mybir as _mybir
    from concourse.bass_utils import run_bass_kernel_spmd as _run

    nc = _bacc.Bacc("TRN2", target_bir_lowering=False, num_devices=1)
    arrays, args = {}, []
    for name in _INS:
        a = _np.ascontiguousarray(inputs[name])
        arrays[f"in_{name}_dram"] = a
        args.append(nc.dram_tensor(f"in_{name}_dram", a.shape, _mybir.dt.from_np(a.dtype),
                                   kind="ExternalInput").ap())
    shape = inputs["x"].shape
    args.append(nc.dram_tensor("out_0_dram", shape, F32, kind="ExternalOutput").ap())
    hybrid_block(nc, *args)
    r = _run(nc, [arrays], core_ids=[0])
    return r.results[0]["out_0_dram"]
```
